# Optimizing a Trainium2 kernel written in Bass

```python
import jax, jax.numpy as jnp
from jax import lax
import numpy as np

D_MODEL = 1024
BATCH = 1
SEQ = 512
DEPTH = 1

N_META = 16
CHUNK = 64
META_PAD = (-N_META) % CHUNK
DN_HEADS = 8
DN_DK = 128
DN_DV = 128
DN_QK = DN_HEADS * DN_DK
DN_VW = DN_HEADS * DN_DV
DN_CONV = 5
SC_WIDTH = 1024
SC_CONV = 3
D_FF = -(-8 * D_MODEL // (3 * 256)) * 256
RMS_EPS = 1e-6
L2_EPS = 1e-6

SPLIT_SIZES = [DN_QK, DN_QK, DN_VW, DN_VW, 2 * DN_HEADS, 2 * DN_HEADS,
               SC_WIDTH, SC_WIDTH, SC_WIDTH, D_MODEL, D_MODEL]
W_IN_COLS = sum(SPLIT_SIZES)
SPLIT_POINTS = list(np.cumsum(SPLIT_SIZES)[:-1].tolist())


def rmsnorm(x, w):
    xf = x.astype(jnp.float32)
    y = xf * lax.rsqrt(jnp.mean(xf * xf, axis=-1, keepdims=True) + RMS_EPS)
    return (y * w.astype(jnp.float32)).astype(x.dtype)

def l2norm(t):
    return t * lax.rsqrt(jnp.sum(t * t, axis=-1, keepdims=True) + L2_EPS)

def depthwise_conv_centred(x, w):
    K, C = w.shape
    r = K // 2
    return lax.conv_general_dilated(
        x, w[:, None, :].astype(x.dtype), window_strides=(1,), padding=[(r, r)],
        dimension_numbers=("NWC", "WIO", "NWC"), feature_group_count=C)

def chunk_gated_delta_rule(q, k, v, g, beta):
    Bsz, T, H, dk = q.shape
    dv = v.shape[-1]
    N = T // CHUNK

    def chunks(t):
        return t.reshape(Bsz, N, CHUNK, H, t.shape[-1]).transpose(0, 1, 3, 2, 4)

    q, k, v = chunks(q), chunks(k), chunks(v)
    g = g.reshape(Bsz, N, CHUNK, H).transpose(0, 1, 3, 2)
    beta = beta.reshape(Bsz, N, CHUNK, H).transpose(0, 1, 3, 2)
    g = jnp.cumsum(g, axis=-1)

    tri = jnp.tril(jnp.ones((CHUNK, CHUNK), dtype=bool))
    strict = jnp.tril(jnp.ones((CHUNK, CHUNK), dtype=bool), -1)
    decay = jnp.exp(jnp.where(tri, g[..., :, None] - g[..., None, :], -jnp.inf))

    kk = jnp.einsum("bnhid,bnhjd->bnhij", k, k)
    lmat = jnp.where(strict, beta[..., :, None] * kk * decay, 0.0)
    a = lmat + jnp.eye(CHUNK, dtype=lmat.dtype)
    rhs = jnp.concatenate([v * beta[..., None], k * (beta * jnp.exp(g))[..., None]], axis=-1)
    sol = lax.linalg.triangular_solve(a, rhs, left_side=True, lower=True, unit_diagonal=True)
    u, w = sol[..., :dv], sol[..., dv:]

    qk = jnp.einsum("bnhid,bnhjd->bnhij", q, k) * decay
    q_dec = q * jnp.exp(g)[..., None]
    g_last = g[..., -1]
    k_dec = k * jnp.exp(g_last[..., None] - g)[..., None]

    xs = tuple(jnp.moveaxis(t, 1, 0) for t in (qk, q_dec, k_dec, u, w, jnp.exp(g_last)))

    def step(S, inp):
        qk_c, qd_c, kd_c, u_c, w_c, gl_c = inp
        v_new = u_c - jnp.einsum("bhcd,bhde->bhce", w_c, S)
        o_c = (jnp.einsum("bhcd,bhde->bhce", qd_c, S)
               + jnp.einsum("bhij,bhje->bhie", qk_c, v_new))
        S = S * gl_c[..., None, None] + jnp.einsum("bhcd,bhce->bhde", kd_c, v_new)
        return S, o_c

    S0 = jnp.zeros((Bsz, H, dk, dv), jnp.float32)
    _, o = lax.scan(step, S0, xs)
    return o.transpose(1, 0, 3, 2, 4).reshape(Bsz, T, H, dv)

def gated_deltanet_bidir(q, k, v, z, b_raw, a_raw, conv_w, A_log, dt_bias, norm_w):
    Bsz, L, _ = q.shape
    f32 = jnp.float32
    qkv = jax.nn.silu(depthwise_conv_centred(jnp.concatenate([q, k, v], axis=-1), conv_w)).astype(f32)
    qc, kc, vc = jnp.split(qkv, [DN_QK, 2 * DN_QK], axis=-1)
    qc = l2norm(qc.reshape(Bsz, L, DN_HEADS, DN_DK)) * (DN_DK ** -0.5)
    kc = l2norm(kc.reshape(Bsz, L, DN_HEADS, DN_DK))
    vc = vc.reshape(Bsz, L, DN_HEADS, DN_DV)
    beta = jax.nn.sigmoid(b_raw.astype(f32)).reshape(Bsz, L, 2, DN_HEADS)
    g = -jnp.exp(A_log.astype(f32)) * jax.nn.softplus(
        a_raw.astype(f32).reshape(Bsz, L, 2, DN_HEADS) + dt_bias.astype(f32))

    def pad(t):
        return jnp.pad(t, [(0, 0), (META_PAD, 0)] + [(0, 0)] * (t.ndim - 2))

    qp, kp, vp, bp, gp = pad(qc), pad(kc), pad(vc), pad(beta), pad(g)
    o_fwd = chunk_gated_delta_rule(qp, kp, vp, gp[:, :, 0], bp[:, :, 0])

    def flip(t):
        return jnp.flip(t, axis=1)

    o_bwd = flip(chunk_gated_delta_rule(flip(qp), flip(kp), flip(vp), flip(gp[:, :, 1]), flip(bp[:, :, 1])))
    o = (o_fwd + o_bwd)[:, META_PAD:]
    o = o * lax.rsqrt(jnp.mean(o * o, axis=-1, keepdims=True) + RMS_EPS) * norm_w.astype(f32)
    o = o * jax.nn.silu(z.reshape(Bsz, L, DN_HEADS, DN_DV).astype(f32))
    return o.reshape(Bsz, L, DN_VW).astype(z.dtype)

def first_inputs(seed: int = 0) -> dict:
    key = jax.random.key(seed)
    ks = jax.random.split(key, 20)
    f32 = jnp.float32

    def nrm(k, shape, scale):
        return jax.random.normal(k, shape, f32) * scale

    x = jax.random.normal(ks[0], (BATCH, SEQ, D_MODEL), f32)
    meta_tokens = nrm(ks[1], (N_META, D_MODEL), 1.0)
    norm1_w = 1.0 + nrm(ks[2], (DEPTH, D_MODEL), 0.02)
    w_in = nrm(ks[3], (DEPTH, D_MODEL, W_IN_COLS), D_MODEL ** -0.5)
    dn_conv_w = nrm(ks[4], (DEPTH, DN_CONV, DN_QK * 2 + DN_VW), DN_CONV ** -0.5)
    A_log = jnp.log(jax.random.uniform(ks[5], (DEPTH, 2, DN_HEADS), f32, 1.0, 16.0))
    dt = jnp.exp(jax.random.uniform(ks[6], (DEPTH, 2, DN_HEADS), f32, np.log(1e-3), np.log(1e-1)))
    dt_bias = dt + jnp.log(-jnp.expm1(-dt))
    dn_norm_w = 1.0 + nrm(ks[7], (DEPTH, DN_DV), 0.02)
    sc_conv_w = nrm(ks[8], (DEPTH, SC_CONV, SC_WIDTH), SC_CONV ** -0.5)
    w_branch_dn = nrm(ks[9], (DEPTH, DN_VW, D_MODEL), DN_VW ** -0.5)
    w_branch_sc = nrm(ks[10], (DEPTH, SC_WIDTH, D_MODEL), SC_WIDTH ** -0.5)
    w_out = nrm(ks[11], (DEPTH, D_MODEL, D_MODEL), D_MODEL ** -0.5)
    norm2_w = 1.0 + nrm(ks[12], (DEPTH, D_MODEL), 0.02)
    w_gate_up = nrm(ks[13], (DEPTH, D_MODEL, 2 * D_FF), D_MODEL ** -0.5)
    w_down = nrm(ks[14], (DEPTH, D_FF, D_MODEL), D_FF ** -0.5)
    final_norm_w = 1.0 + nrm(ks[15], (D_MODEL,), 0.02)
    return {"x": x, "meta_tokens": meta_tokens, "norm1_w": norm1_w, "w_in": w_in,
            "dn_conv_w": dn_conv_w, "A_log": A_log, "dt_bias": dt_bias, "dn_norm_w": dn_norm_w,
            "sc_conv_w": sc_conv_w, "w_branch_dn": w_branch_dn, "w_branch_sc": w_branch_sc,
            "w_out": w_out, "norm2_w": norm2_w, "w_gate_up": w_gate_up, "w_down": w_down,
            "final_norm_w": final_norm_w}

def first_block(x, meta_tokens, norm1_w, w_in, dn_conv_w, A_log, dt_bias, dn_norm_w,
              sc_conv_w, w_branch_dn, w_branch_sc, w_out, norm2_w, w_gate_up, w_down,
              final_norm_w):
    Bsz = x.shape[0]
    meta = jnp.broadcast_to(meta_tokens[None].astype(x.dtype), (Bsz, N_META, x.shape[-1]))
    h_res = jnp.concatenate([meta, x], axis=1)
    for l in range(DEPTH):
        h = rmsnorm(h_res, norm1_w[l])
        proj = h @ w_in[l]
        (q, k, v, z, b_raw, a_raw, sc_b, sc_c, sc_x, gate_a, gate_b) = jnp.split(proj, SPLIT_POINTS, axis=-1)
        o_dn = gated_deltanet_bidir(q, k, v, z, b_raw, a_raw, dn_conv_w[l], A_log[l], dt_bias[l], dn_norm_w[l])
        y_a = o_dn @ w_branch_dn[l]
        y_b = (sc_b * depthwise_conv_centred(sc_c * sc_x, sc_conv_w[l])) @ w_branch_sc[l]
        merged = jax.nn.sigmoid(gate_a) * y_a + jax.nn.sigmoid(gate_b) * y_b
        h_res = h_res + merged @ w_out[l]
        h2 = rmsnorm(h_res, norm2_w[l])
        gu = h2 @ w_gate_up[l]
        h_res = h_res + (jax.nn.silu(gu[..., :D_FF]) * gu[..., D_FF:]) @ w_down[l]
    out = rmsnorm(h_res, final_norm_w)
    return out[:, N_META:]


DEPTH_2 = 2

EPS_RMS = 1e-6
EPS_LN = 1e-5
W_CONV = D_MODEL
CONV_K = 31
W_POOL = D_MODEL
POOL_WINDOWS = (2, 4, 8, 16)
POOL_GROUPS = len(POOL_WINDOWS)
POOL_GW = W_POOL // POOL_GROUPS
W_EVEN_IN = 3 * W_CONV + 2 * W_POOL
W_EVEN_MIX = W_CONV + W_POOL
LRU_HEADS = 12
LRU_HD = 128
W_LRU = LRU_HEADS * LRU_HD
LRU_CONV_K = 4
LRU_C = 8.0
N_EVEN = (DEPTH_2 + 1) // 2
N_ODD = DEPTH_2 // 2


def rmsnorm_2(x, g):
    xf = x.astype(jnp.float32)
    y = xf * lax.rsqrt(jnp.mean(xf * xf, axis=-1, keepdims=True) + EPS_RMS)
    return (y * g.astype(jnp.float32)).astype(x.dtype)

def layernorm(x, g, b):
    xf = x.astype(jnp.float32)
    mu = jnp.mean(xf, axis=-1, keepdims=True)
    var = jnp.mean(jnp.square(xf - mu), axis=-1, keepdims=True)
    y = (xf - mu) * lax.rsqrt(var + EPS_LN)
    return (y * g.astype(jnp.float32) + b.astype(jnp.float32)).astype(x.dtype)

def causal_depthwise_conv(x, w, b):
    k = w.shape[0]
    y = lax.conv_general_dilated(
        x, w[:, None, :].astype(x.dtype), window_strides=(1,), padding=[(k - 1, 0)],
        dimension_numbers=("NWC", "WIO", "NWC"), feature_group_count=x.shape[-1])
    return y + b.astype(x.dtype)

def multiscale_pool_diff(v):
    bsz, t, _ = v.shape
    vf = v.astype(jnp.float32)
    cs_pad = jnp.pad(jnp.cumsum(vf, axis=1), ((0, 0), (1, 0), (0, 0)))
    pos = jnp.arange(1, t + 1, dtype=jnp.float32)
    outs = []
    for g, w in enumerate(POOL_WINDOWS):
        seg = cs_pad[:, :, g * POOL_GW:(g + 1) * POOL_GW]
        upper = seg[:, 1:]
        lower = jnp.pad(seg[:, :t - w + 1], ((0, 0), (w - 1, 0), (0, 0)))
        cnt = jnp.minimum(pos, jnp.float32(w))[None, :, None]
        outs.append((upper - lower) / cnt)
    return jnp.concatenate(outs, axis=-1) - vf

def even_mixer(h, w_in, conv_w, conv_b, ln_g, ln_b, pool_w, pool_b, pool_scale, w_out):
    bsz, t, _ = h.shape
    p = jnp.einsum("btd,dn->btn", h, w_in)
    a_val, a_glu, a_gate, b_val, b_gate = jnp.split(
        p, [W_CONV, 2 * W_CONV, 3 * W_CONV, 3 * W_CONV + W_POOL], axis=-1)
    u = a_val * jax.nn.sigmoid(a_glu)
    u = causal_depthwise_conv(u, conv_w, conv_b)
    u = jax.nn.silu(layernorm(u, ln_g, ln_b))
    ya = u * jax.nn.silu(a_gate)
    d = multiscale_pool_diff(b_val).reshape(bsz, t, POOL_GROUPS, POOL_GW)
    d = jnp.einsum("btgc,gce->btge", d, pool_w.astype(jnp.float32)) + pool_b.astype(jnp.float32)
    yb = (d.reshape(bsz, t, W_POOL) * pool_scale.astype(jnp.float32)).astype(h.dtype)
    yb = yb * jax.nn.silu(b_gate)
    y = jnp.concatenate([ya, yb], axis=-1)
    return jnp.einsum("btn,nd->btd", y, w_out)

def _lin_combine(c1, c2):
    a1, b1 = c1
    a2, b2 = c2
    return a1 * a2, a2 * b1 + b2

def odd_mixer(h, w_in, conv_w, conv_b, w_rg, b_rg, w_ig, b_ig, lam, w_out):
    bsz, t, _ = h.shape
    p = jnp.einsum("btd,dn->btn", h, w_in)
    xr, gate = jnp.split(p, [W_LRU], axis=-1)
    xc = causal_depthwise_conv(xr, conv_w, conv_b)
    xh = xc.reshape(bsz, t, LRU_HEADS, LRU_HD)
    r = jax.nn.sigmoid(jnp.einsum("bthi,hij->bthj", xh, w_rg).reshape(bsz, t, W_LRU).astype(jnp.float32)
                       + b_rg.astype(jnp.float32))
    i = jax.nn.sigmoid(jnp.einsum("bthi,hij->bthj", xh, w_ig).reshape(bsz, t, W_LRU).astype(jnp.float32)
                       + b_ig.astype(jnp.float32))
    log_a = -LRU_C * r * jax.nn.softplus(-lam.astype(jnp.float32))
    a = jnp.exp(log_a)
    mult = jnp.sqrt(-jnp.expm1(2.0 * log_a))
    bterm = mult * (i * xc.astype(jnp.float32))
    _, hs = lax.associative_scan(_lin_combine, (a, bterm), axis=1)
    y = hs.astype(h.dtype) * jax.nn.silu(gate)
    return jnp.einsum("btn,nd->btd", y, w_out)

def second_inputs(seed: int = 0) -> dict:
    key = jax.random.key(seed)
    ks = iter(jax.random.split(key, 32))
    f32 = jnp.float32

    def nrm(shape, scale):
        return jax.random.normal(next(ks), shape, f32) * scale

    x = jax.random.normal(next(ks), (BATCH, SEQ, D_MODEL), f32)
    a0 = jax.random.uniform(next(ks), (N_ODD, W_LRU), f32, 0.9, 0.999)
    s = a0 ** (1.0 / LRU_C)
    lru_lambda = jnp.log(s) - jnp.log1p(-s)
    return {
        "x": x,
        "norm_even": 1.0 + nrm((N_EVEN, D_MODEL), 0.02),
        "w_in_even": nrm((N_EVEN, D_MODEL, W_EVEN_IN), D_MODEL ** -0.5),
        "conv_a_w": nrm((N_EVEN, CONV_K, W_CONV), CONV_K ** -0.5),
        "conv_a_b": nrm((N_EVEN, W_CONV), 0.01),
        "ln_a_g": 1.0 + nrm((N_EVEN, W_CONV), 0.02),
        "ln_a_b": nrm((N_EVEN, W_CONV), 0.01),
        "pool_w": nrm((N_EVEN, POOL_GROUPS, POOL_GW, POOL_GW), POOL_GW ** -0.5),
        "pool_b": nrm((N_EVEN, POOL_GROUPS, POOL_GW), 0.01),
        "pool_scale": 1.0 + nrm((N_EVEN, W_POOL), 0.1),
        "w_out_even": nrm((N_EVEN, W_EVEN_MIX, D_MODEL), W_EVEN_MIX ** -0.5),
        "norm_odd": 1.0 + nrm((N_ODD, D_MODEL), 0.02),
        "w_in_odd": nrm((N_ODD, D_MODEL, 2 * W_LRU), D_MODEL ** -0.5),
        "conv_c_w": nrm((N_ODD, LRU_CONV_K, W_LRU), LRU_CONV_K ** -0.5),
        "conv_c_b": nrm((N_ODD, W_LRU), 0.01),
        "w_rg": nrm((N_ODD, LRU_HEADS, LRU_HD, LRU_HD), LRU_HD ** -0.5),
        "b_rg": nrm((N_ODD, W_LRU), 0.01),
        "w_ig": nrm((N_ODD, LRU_HEADS, LRU_HD, LRU_HD), LRU_HD ** -0.5),
        "b_ig": nrm((N_ODD, W_LRU), 0.01),
        "lru_lambda": lru_lambda,
        "w_out_odd": nrm((N_ODD, W_LRU, D_MODEL), W_LRU ** -0.5),
        "final_norm": 1.0 + nrm((D_MODEL,), 0.02),
    }

def second_block(x, norm_even, w_in_even, conv_a_w, conv_a_b, ln_a_g, ln_a_b, pool_w, pool_b,
              pool_scale, w_out_even, norm_odd, w_in_odd, conv_c_w, conv_c_b, w_rg, b_rg,
              w_ig, b_ig, lru_lambda, w_out_odd, final_norm):
    h = x
    for layer in range(DEPTH_2):
        if layer % 2 == 0:
            j = layer // 2
            h = h + even_mixer(rmsnorm_2(h, norm_even[j]), w_in_even[j], conv_a_w[j], conv_a_b[j],
                               ln_a_g[j], ln_a_b[j], pool_w[j], pool_b[j], pool_scale[j],
                               w_out_even[j])
        else:
            j = layer // 2
            h = h + odd_mixer(rmsnorm_2(h, norm_odd[j]), w_in_odd[j], conv_c_w[j], conv_c_b[j],
                              w_rg[j], b_rg[j], w_ig[j], b_ig[j], lru_lambda[j], w_out_odd[j])
    return rmsnorm_2(h, final_norm)


def setup_inputs(seed=0):
    out = dict(first_inputs(seed))
    for name, value in second_inputs(seed + 1).items():
        if name != "x":
            out[name + "_2"] = value
    return out


def reference(
    x, meta_tokens, norm1_w, w_in, dn_conv_w, A_log, dt_bias, dn_norm_w, sc_conv_w, w_branch_dn,
    w_branch_sc, w_out, norm2_w, w_gate_up, w_down, final_norm_w, norm_even_2, w_in_even_2,
    conv_a_w_2, conv_a_b_2, ln_a_g_2, ln_a_b_2, pool_w_2, pool_b_2, pool_scale_2, w_out_even_2,
    norm_odd_2, w_in_odd_2, conv_c_w_2, conv_c_b_2, w_rg_2, b_rg_2, w_ig_2, b_ig_2,
    lru_lambda_2, w_out_odd_2, final_norm_2,
):
    x = first_block(
        x, meta_tokens, norm1_w, w_in, dn_conv_w, A_log, dt_bias, dn_norm_w, sc_conv_w,
        w_branch_dn, w_branch_sc, w_out, norm2_w, w_gate_up, w_down, final_norm_w,
    )
    return second_block(
        x, norm_even_2, w_in_even_2, conv_a_w_2, conv_a_b_2, ln_a_g_2, ln_a_b_2, pool_w_2,
        pool_b_2, pool_scale_2, w_out_even_2, norm_odd_2, w_in_odd_2, conv_c_w_2, conv_c_b_2,
        w_rg_2, b_rg_2, w_ig_2, b_ig_2, lru_lambda_2, w_out_odd_2, final_norm_2,
    )


_drawn_inputs = setup_inputs


def setup_inputs(seed=0):
    import zlib

    import numpy as np

    out = dict(_drawn_inputs(seed))
    spreads = {}
    factors = {'dn_norm_w': 7.421,
     'norm2_w': 3.879,
     'norm_even_2': 4.611,
     'conv_a_b_2': 8.0,
     'ln_a_g_2': 8.0,
     'ln_a_b_2': 33.067,
     'pool_b_2': 8.0,
     'norm_odd_2': 6.127,
     'b_rg_2': 64.0,
     'b_ig_2': 47.006,
     'final_norm_2': 7.984,
     'conv_c_b_2': 8.0}
    for name, (base, spread) in spreads.items():
        noise = np.random.default_rng([zlib.crc32(name.encode()), seed]).standard_normal(out[name].shape)
        drawn = base * np.exp(spread * noise) if base else spread * noise
        out[name] = __import__('jax').numpy.asarray(drawn.astype(out[name].dtype))
    for name, factor in factors.items():
        out[name] = (out[name] * factor).astype(out[name].dtype)
    return out
```

```python
from contextlib import ExitStack

import numpy as np
import concourse.bass as bass
from concourse import mybir

F32 = mybir.dt.float32
F32R = mybir.dt.float32r
BF16 = mybir.dt.bfloat16
ALU = mybir.AluOpType
ACT = mybir.ActivationFunctionType

P = 128
D = 1024
KT = D // P
SEQ = 512
META = 16
T1 = META + SEQ
HALF = T1 // 2
H = 8
CH = 128
NCH = SEQ // CH
FF = 2816
FT = FF // P
LW = 1536
LT = LW // P
WT = 8
RAW = 4
EPS = 1e-6
NEG = -30000.0
LEVELS = [1, 2, 4, 8, 16, 32, 64]

UNITS = [("q", H), ("k", H), ("v", H), ("z", KT), ("sc", 3 * KT), ("bsc", 2 * KT), ("bdn", 2 * KT),
         ("out", KT), ("gu", 2 * FT), ("down", 3 * KT), ("glu", 2 * KT), ("bval", KT), ("pool", 4),
         ("bgate", KT), ("agate", KT), ("mix", 2 * KT), ("xr", LT), ("lru", 4), ("lgate", LT),
         ("lout", 2 * KT)]
BASE = {}
NU = 0
for _name, _n in UNITS:
    BASE[_name] = NU
    NU += _n
    assert _n % RAW == 0

PARAMS = [("norm1", KT, 1), ("cq", H, 5), ("ck", H, 5), ("cv", H, 5), ("sc", KT, 3), ("dnn", 1, 1),
          ("norm2", KT, 1), ("fin1", KT, 1), ("even", KT, 1), ("ca", KT, 31), ("cab", KT, 1),
          ("lng", KT, 1), ("lnb", KT, 1), ("pb", KT, 1), ("psc", KT, 1), ("odd", KT, 1), ("cc", LT, 4),
          ("ccb", LT, 1), ("brg", LT, 1), ("big", LT, 1), ("lam", LT, 1), ("fin2", KT, 1)]
PAR = {}
NPAR = 0
for _name, _n, _k in PARAMS:
    PAR[_name] = (NPAR, _n, _k)
    NPAR += _n * _k
NPAR_PAD = NPAR + (-NPAR) % 8

CONSTS = ["ident", "ones", "ones128", "mean1024", "mean128", "uf", "vf", "ub", "vb"] + [f"m{b}" for b in LEVELS]
CIDX = {n: i for i, n in enumerate(CONSTS)}
POOLW = [2, 4, 8, 16]


class Steps:

    def __init__(self, sem, names):
        self.sem, self.names, self.n = sem, list(names), len(names)
        self.at = {k: i for i, k in enumerate(self.names)}
        self.next = 0
        assert len(self.at) == self.n

    def open(self, e):
        e.sem_inc(self.sem, self.n)

    def done(self, ins, step):
        assert self.names[self.next % self.n] == step, (step, self.names[self.next % self.n])
        self.next += 1
        ins.then_inc(self.sem, 1)

    def count(self, it, step, back=0):
        return it * self.n + (1 - back) * self.n + self.at[step] + 1


def build(nc, a, out):
    ctx = ExitStack()
    with ctx:
        def sem(name):
            return ctx.enter_context(nc.semaphore(name))

        start = nc.sbuf_base + (-nc.sbuf_base) % 32
        top = [start]

        def at(name, shape, offset, dt=F32):
            return nc.alloc_sbuf_tensor_at(name, shape, dt, offset=offset)

        def put(name, shape, dt=F32):
            n = int(np.prod(shape[1:])) * (2 if dt == BF16 else 4)
            t = at(name, shape, top[0], dt)
            top[0] += n + (-n) % 32
            return t

        w_raw = put("w_raw", [P, RAW, WT * P])
        w_hi = put("w_hi", [P, 2, WT * P], F32R)
        w_lo = put("w_lo", [P, 2, WT * P], F32R)
        h_hi = put("h_hi", [P, KT, T1], F32R)
        h_lo = put("h_lo", [P, KT, T1], F32R)
        par = put("par", [P, NPAR_PAD])
        cf = put("cf", [P, len(CONSTS), P])
        cb = put("cb", [P, 3, P], BF16)
        small = put("small", [P, 128])
        z0 = top[0]
        K16 = 16384

        def z(name, shape, off, dt=F32):
            n = int(np.prod(shape[1:])) * 4
            assert z0 + off + n <= nc.sbuf_usable_end, (name, z0 + off + n, nc.sbuf_usable_end)
            return at(name, shape, z0 + off, dt)

        oT = z("oT", [P, H, SEQ], 0)
        qT = z("qT", [P, H, T1], K16)
        kT = z("kT", [P, H, T1], K16 + 16896)
        dl = K16 + 2 * 16896
        x_in = z("x_in", [P, KT, T1], dl)
        v_tok = z("v_tok", [P, NCH, H, P], dl)
        k_tok = z("k_tok", [P, NCH, H, P], dl + K16)
        v_met = z("v_met", [P, H, P], dl + 2 * K16)
        k_met = z("k_met", [P, H, P], dl + 2 * K16 + 4096)
        st = z("st", [P, 2, H, P], dl + 2 * K16 + 8192)
        tb = dl + 2 * K16 + 16384
        NB = NCH + 1
        beta = z("beta", [P, NB, 2 * H], tb)
        gdec = z("gdec", [P, NB, 2 * H], tb + 320)
        ecol = z("ecol", [P, NB, 2 * H], tb + 640)
        kcol = z("kcol", [P, NB, 2 * H], tb + 960)
        lcol = z("lcol", [P, NB, 2 * H], tb + 1280)
        tmpc = z("tmpc", [P, 4, NB * 2 * H], 13312)
        wk = tb + 1600
        vT = z("vT", [P, H, T1], wk)
        HG = 4
        work = {}
        for _i, _n in enumerate(["dec", "a", "e", "x", "xt", "tt", "kc", "eg"]):
            work[_n] = z(f"wk_{_n}", [P, 2, HG, P], wk + _i * 4096)
        cin = z("cin", [P, 2, T1 + 4], 0)
        cacc = z("cacc", [P, 2, T1], 4256)
        sqv = z("sqv", [P, 2, T1], 8704)
        rrow = z("rrow", [P, T1], dl + 2 * K16 + 8192)
        rbuf = z("rbuf", [P, 4, T1], dl + 2 * K16 + 8192)
        hf0 = z("hf0", [P, 2, T1], wk)
        wba = z("wba", [P, KT, 32], wk + 20000)
        wba_hi = z("wba_hi", [P, KT, 32], wk + 20000 + 1024, F32R)
        wba_lo = z("wba_lo", [P, KT, 32], wk + 20000 + 2048, F32R)

        zs = z("zs", [P, KT, SEQ], K16)
        od_hi = z("od_hi", [P, KT, SEQ], 2 * K16, F32R)
        od_lo = z("od_lo", [P, KT, SEQ], 3 * K16, F32R)
        sc_hi = z("sc_hi", [P, KT, SEQ], 4 * K16, F32R)
        sc_lo = z("sc_lo", [P, KT, SEQ], 5 * K16, F32R)
        m1 = z("m1", [P, KT, SEQ], 6 * K16)
        me_hi = z("me_hi", [P, KT, SEQ], 0, F32R)
        me_lo = z("me_lo", [P, KT, SEQ], K16, F32R)
        tz = 7 * K16
        tmp = z("tmp", [P, 8, SEQ + 32], tz)
        x_res = z("x_res", [P, KT, SEQ], 4 * K16)
        x = z("x", [P, KT, SEQ], 6 * K16)
        y_hi = z("y_hi", [P, FT, SEQ], 0, F32R)
        y_lo = z("y_lo", [P, FT, SEQ], FT * SEQ * 4, F32R)
        uc = z("uc", [P, KT, SEQ], 0)
        mx_hi = z("mx_hi", [P, 2 * KT, SEQ], K16, F32R)
        mx_lo = z("mx_lo", [P, 2 * KT, SEQ], 3 * K16, F32R)
        yb = z("yb", [P, KT, SEQ], 5 * K16)
        xc = z("xc", [P, LT, SEQ], 0)
        L24 = LT * SEQ * 4
        xc_hi = z("xc_hi", [P, LT, SEQ], L24, F32R)
        xc_lo = z("xc_lo", [P, LT, SEQ], 2 * L24, F32R)
        hs = z("hs", [P, LT, SEQ], 3 * L24)

        ps = ctx.enter_context(nc.psum_tensor("ps", [P, 8, 512], F32))

        def cmat(name):
            return cf[:, CIDX[name], :]

        def pcol(name, tile, tap=0):
            o, n, k = PAR[name]
            return par[:, o:o + n * k].rearrange("p (n k) -> p n k", k=k)[:, tile, tap:tap + 1]

        eps_col = small[:, 124:125]
        s_raw = [sem(f"s_raw{j}") for j in range(RAW)]
        s_hi, s_lo, s_pe = sem("s_hi"), sem("s_lo"), sem("s_pe")
        s_x, s_cst, s_xr, s_out = sem("s_x"), sem("s_cst"), sem("s_xr"), sem("s_out")
        s_zero = sem("s_zero")
        ticks = {}

        def wait(e, st_, it, step, back=0):
            n = st_.count(it, step, back)
            e.wait_ge(st_.sem, n)
            settle(e, n)

        def settle(e, n):
            if not isinstance(n, int) and e in ticks:
                e.reg_add(ticks[e], ticks[e], 1)

        def loop(e, n, body, iter0=0):
            if n == 1:
                body(iter0)
            else:
                with e.Fori(iter0, iter0 + n) as it:
                    body(it)

        def round_unit(e, u, c):
            j = c % RAW
            div = (u - j) if isinstance(u, int) else None
            n = 16 * (div // RAW + 1) if div is not None else (u - j) * (16 // RAW) + 16
            e.wait_ge(s_raw[j], n)
            if not (isinstance(u, int) and u < 2):
                e.wait_ge(s_pe, u - 1)
            settle(e, n)
            e.activation(w_hi[:, j % 2, :], w_raw[:, j, :], ACT.Copy).then_inc(s_hi, 1)

        def split_unit(e, u, c):
            e.wait_ge(s_hi, u + 1)
            settle(e, u)
            e.tensor_tensor(w_lo[:, c % 2, :], w_raw[:, c % RAW, :], w_hi[:, c % 2, :].bitcast(F32),
                            ALU.subtract).then_inc(s_lo, 1)

        def ahead(e, stage, it, per, j, fn):
            u = it * per + (BASE[stage] + j + 2)
            if not (isinstance(u, int) and u >= NU):
                fn(e, u, j + 2)

        def unit(e, stage, it, per, j, outs, xh, xl, tiles, first, last):
            e.wait_ge(s_lo, it * per + (BASE[stage] + j + 1))
            s = j % 2
            for n, (t, k) in enumerate(tiles):
                wh, wl = w_hi[:, s, t * P:(t + 1) * P], w_lo[:, s, t * P:(t + 1) * P]
                for w, r, p3 in ((wh, xh, 0), (wh, xl, 1), (wl, xh, 2)):
                    for v, o in enumerate(outs):
                        m = e.matmul(o, w, r(k, v), start=(first and n == 0 and p3 == 0),
                                     stop=(last and n == len(tiles) - 1 and p3 == 2))
            return m

        def pe_done(e, stage, it, per, j):
            n = it * per + (BASE[stage] + j + 1)
            e.wait_ge(s_pe, n)
            settle(e, n)

        K8 = [(t, t) for t in range(KT)]

        def h_views(hi_lo, lo_tok=META):
            return lambda k, v: hi_lo[:, k, lo_tok:lo_tok + SEQ]

        class Stage:

            def __init__(self, name, before):
                self.name, self.before, self.log = name, before, {}
                stages.append(self)

            def steps(self, eng, names, iters=1):
                s = Steps(sem(f"s_{self.name}_{eng}"), names)
                s.iters = iters
                self.log[eng] = s
                return s

            def wait_whole(self, e, engs=("act", "dve", "pool", "pe")):
                for g in engs:
                    if g in self.log:
                        e.wait_ge(self.log[g].sem, (self.log[g].iters + 1) * self.log[g].n)

            def begin(self, e, eng):
                if eng in self.log:
                    self.log[eng].open(e)
                if self.before is not None:
                    self.before.wait_whole(e)

            def on(self, e, eng, it, step, back=0):
                wait(e, self.log[eng], it, step, back)

            def did(self, eng, ins, step):
                self.log[eng].done(ins, step)

            def sp(self, e): pass
            def pe(self, e): pass
            def act(self, e): pass
            def dve(self, e): pass
            def pool(self, e): pass

        class Linear(Stage):

            def __init__(self, name, before, n, m, units, banks, freed, prog, width=((META, T1),), final=False,
                         inputs=None, start=None):
                super().__init__(name, before)
                self.n, self.m, self.units, self.banks, self.freed = n, m, units, banks, freed
                self.prog, self.width, self.final, self.inputs, self.start = prog, width, final, inputs, start or {}
                self.per = m * len(units)
                self.order = {}
                for eng in ("act", "dve", "pool", "pe"):
                    now = [q for q in prog if q[0] == eng and len(q) == 4]
                    late = [q for q in prog if q[0] == eng and len(q) == 5 and q[4] != "end"]
                    ends = [q for q in prog if q[0] == eng and len(q) == 5 and q[4] == "end"]
                    order = []
                    for j in range(m):
                        order += [(q, j) for q in now] + ([(q, j - 1) for q in late] if j else [])
                        order.append((None, j))
                    order += [(q, m - 1) for q in late] + [(q, m - 1) for q in ends]
                    self.order[eng] = order
                    if now or late or ends:
                        self.steps(eng, [(q[1], j) for q, j in order if q], n)

            def back(self, j, k):
                assert k <= self.m
                return ((j - k) % self.m, int(j < k))

            def await_(self, e, it, j, what):
                if what[0] == "out":
                    u = max(i for i, q in enumerate(self.units) if q[0] == what[1])
                    n = it * self.per + (BASE[self.name] + j * len(self.units) + u + 1)
                    e.wait_ge(s_pe, n)
                    settle(e, n)
                else:
                    eng, step, k = what
                    jj, b = (self.m - 1, 1) if k == "end" else self.back(j, k)
                    self.on(e, eng, it, (step, jj), b)

            def emit(self, e, eng, it, q, j):
                for w in q[2]:
                    self.await_(e, it, j, w)
                self.did(eng, q[3](e, it * self.m + j, j), (q[1], j))

            def side(self, e, eng, prepare):
                self.begin(e, eng)
                if eng in self.start:
                    self.start[eng](e)
                nu = len(self.units)
                before_gemm = [q for q in self.prog if q[0] == eng and q[1].startswith("pre")]

                def body(it):
                    done = set()

                    def ahead(j):
                        if j in done or prepare is None:
                            return
                        done.add(j)
                        for u in range(nu):
                            c = j * nu + u + 2
                            w = it * self.per + (BASE[self.name] + c)
                            if not (isinstance(w, int) and w >= NU):
                                prepare(e, w, c)
                    for q, j in self.order[eng]:
                        if q is None or not q in before_gemm:
                            ahead(j if q is None or len(q) == 4 else min(j + 1, self.m - 1))
                        if q is not None:
                            self.emit(e, eng, it, q, j)
                self.run(e, body)

            def run(self, e, body):
                loop(e, self.n - int(self.final), body)
                if self.final:
                    body(self.n - 1)

            def act(self, e):
                self.side(e, "act", round_unit)

            def dve(self, e):
                self.side(e, "dve", None)

            def pool(self, e):
                self.side(e, "pool", split_unit)

            def pe(self, e):
                if "pe" in self.log:
                    self.log["pe"].open(e)
                (self.inputs or self.before).wait_whole(e, ("act", "dve", "pool"))
                if self.inputs is not None:
                    self.before.wait_whole(e, ("act", "dve"))
                nu = len(self.units)

                def body(it):
                    for j in range(self.m):
                        for u, (o, hi, lo, tiles, first, last) in enumerate(self.units):
                            if first:
                                self.await_(e, it, j, self.freed[o])
                            outs = self.banks(j, o)
                            width = self.width[o] if isinstance(self.width, dict) else self.width
                            if len(tiles) and isinstance(tiles[0], list):
                                groups = tiles
                            else:
                                groups = [tiles]
                            e.wait_ge(s_lo, it * self.per + (BASE[self.name] + j * nu + u + 1))
                            s = (j * nu + u) % 2
                            for g, tl in enumerate(groups):
                                gouts = outs if len(groups) == 1 else outs[g]
                                for n, (t, k) in enumerate(tl):
                                    wh, wl = w_hi[:, s, t * P:(t + 1) * P], w_lo[:, s, t * P:(t + 1) * P]
                                    for p3, (w, r) in enumerate(((wh, hi), (wh, lo), (wl, hi))):
                                        for v, ov in enumerate(gouts):
                                            t0, t1 = width[v]
                                            kk = k(j) if callable(k) else k
                                            mm = e.matmul(ov, w, r[:, kk, t0:t1], start=(first and n == 0 and p3 == 0),
                                                          stop=(last and n == len(tl) - 1 and p3 == 2))
                            mm.then_inc(s_pe, 1)
                        for q, jj in self.order["pe"]:
                            if q is not None and jj == j:
                                self.emit(e, "pe", it, q, j)
                self.run(e, body)

        K8 = [(t, t) for t in range(KT)]
        stages = []

        def dve_w(step):
            return ("dve", step, 0)

        class Prologue(Stage):
            def __init__(self):
                super().__init__("pro", None)
                self.steps("dve", ["halo0", "halo1", "wlo"])
                self.steps("act", ["whi"])

            def act(self, e):
                self.begin(e, "act")
                e.dma_start(par[:], a["par"]).then_inc(s_cst, 16)
                e.dma_start(cf[:], a["cf"]).then_inc(s_cst, 16)
                e.dma_start(cb[:], a["cb"]).then_inc(s_cst, 16)
                e.dma_start(small[:], a["small"]).then_inc(s_cst, 16)
                e.dma_start(wba[:], a["wba"]).then_inc(s_cst, 16)
                e.wait_ge(s_cst, 80)
                self.did("act", e.activation(wba_hi[:], wba[:], ACT.Copy), "whi")
                for u in range(2):
                    round_unit(e, u, u)

            def pool(self, e):
                for u in range(2):
                    split_unit(e, u, u)

            def dve(self, e):
                self.begin(e, "dve")
                self.did("dve", e.memset(cin[:, :, 0:2], 0.0), "halo0")
                self.did("dve", e.memset(cin[:, :, T1 + 2:T1 + 4], 0.0), "halo1")
                self.on(e, "act", 0, "whi")
                self.did("dve", e.tensor_tensor(wba_lo[:], wba[:], wba_hi[:].bitcast(F32), ALU.subtract), "wlo")

            def sp(self, e):
                e.dma_start(x_in[:], a["x"]).then_inc(s_x, 16)
                for u in range(RAW):
                    e.dma_start(w_raw[:, u, :], a["w"][u]).then_inc(s_raw[u], 16)

                def body(it):
                    for j in range(RAW):
                        e.wait_ge(s_lo, it * RAW + (j + 1 - RAW))
                        e.dma_start(w_raw[:, j, :], a["w"][it * RAW + j]).then_inc(s_raw[j], 16)
                loop(e, NU // RAW - 1, body, 1)

        class Norm(Stage):

            def __init__(self, name, before, src, w, tokens, plain=None, hf=None, sq=None, rr=None):
                super().__init__(name, before)
                self.src, self.w, self.t, self.plain = src, w, tokens, plain
                self.views = [(0, HALF), (HALF, T1)] if tokens == T1 else [(0, tokens)]
                self.hf = hf if hf is not None else tmp[:, 0:2, 0:SEQ]
                self.sq = sq if sq is not None else tmp[:, 2:4, 0:SEQ]
                self.rr = rr if rr is not None else tmp[:, 4, 0:SEQ]
                self.o = 0 if tokens == T1 else META
                split = plain is None
                self.steps("act", [("sq", k) for k in range(KT)] + ["rt"] + [("hi", k) for k in range(KT) if split])
                self.steps("pe", [("ss", k) for k in range(KT)])
                self.steps("dve", ["r"] + [("h", k) for k in range(KT)])
                if split:
                    self.steps("pool", [("lo", k) for k in range(KT)])

            def loaded(self, e):
                if self.src is x_in:
                    e.wait_ge(s_x, 16)
                    e.wait_ge(s_cst, 80)

            def act(self, e):
                self.begin(e, "act")
                self.loaded(e)
                for k in range(KT):
                    if k > 1:
                        self.on(e, "pe", 0, ("ss", k - 2))
                    self.did("act", e.activation(self.sq[:, k % 2, 0:self.t], self.src[:, k, 0:self.t], ACT.Square), ("sq", k))
                self.on(e, "pe", 0, ("ss", KT - 1))
                nb, w = len(self.views), self.views[0][1]
                self.did("act", e.activation(self.rr[:, 0:self.t].rearrange("p (b n) -> p b n", b=nb), ps[:, 4:4 + nb, 0:w],
                                             ACT.Sqrt, bias=eps_col), "rt")
                if self.plain is None:
                    for k in range(KT):
                        self.on(e, "dve", 0, ("h", k))
                        self.did("act", e.activation(h_hi[:, k, self.o:self.o + self.t], self.hf[:, k % 2, 0:self.t], ACT.Copy), ("hi", k))

            def pe(self, e):
                self.begin(e, "pe")
                self.loaded(e)
                for k in range(KT):
                    self.on(e, "act", 0, ("sq", k))
                    for b, (lo, hi) in enumerate(self.views):
                        mm = e.matmul(ps[:, 4 + b, 0:hi - lo], cmat("mean1024"), self.sq[:, k % 2, lo:hi], start=(k == 0), stop=(k == KT - 1))
                    self.did("pe", mm, ("ss", k))

            def dve(self, e):
                self.begin(e, "dve")
                self.loaded(e)
                self.on(e, "act", 0, "rt")
                self.did("dve", e.reciprocal(self.rr[:, 0:self.t], self.rr[:, 0:self.t]), "r")
                self.on(e, "dve", 0, "r")
                for k in range(KT):
                    if self.plain is None and k > 1:
                        self.on(e, "pool", 0, ("lo", k - 2))
                    dst = self.hf[:, k % 2, 0:self.t] if self.plain is None else self.plain[:, k, :]
                    self.did("dve", e.scalar_tensor_tensor(dst, self.src[:, k, 0:self.t], pcol(self.w, k), self.rr[:, 0:self.t], ALU.mult, ALU.mult), ("h", k))

            def pool(self, e):
                if self.plain is None:
                    self.begin(e, "pool")
                    for k in range(KT):
                        self.on(e, "act", 0, ("hi", k))
                        o = self.o
                        self.did("pool", e.tensor_tensor(h_lo[:, k, o:o + self.t], self.hf[:, k % 2, 0:self.t], h_hi[:, k, o:o + self.t].bitcast(F32), ALU.subtract), ("lo", k))

        two = ((0, HALF), (HALF, T1))

        def pair(v):
            return v.rearrange("p (b n) -> p b n", b=2)

        def qkv(name, before, cw, dst, side, side_ones):
            prog = []
            if side is not None:
                bias = small[:, 125:126] if side_ones == "ones128" else eps_col
                prog += [
                    ("act", "presq", [("pe", "ss", 2)], lambda e, i, j: e.activation(sqv[:, j % 2, :], side[:, i, :], ACT.Square)),
                    ("pe", "ss", [("act", "presq", 0), ("act", "rc", 1)], lambda e, i, j: [
                        e.matmul(ps[:, 4 + v, 0:HALF], cmat(side_ones), sqv[:, j % 2, v * HALF:(v + 1) * HALF], start=True, stop=True)
                        for v in range(2)][-1]),
                    ("act", "rc", [("pe", "ss", 0), ("pool", "nrm", "end")], lambda e, i, j: e.activation(
                        pair(rbuf[:, j, :]), ps[:, 4:6, 0:HALF], ACT.Copy), 1),
                    ("act", "rt", [("act", "rc", 0)], lambda e, i, j: e.activation(rbuf[:], rbuf[:], ACT.Sqrt, bias=bias), "end"),
                    ("dve", "rec", [("act", "rt", 0)], lambda e, i, j: e.reciprocal(rbuf[:], rbuf[:]), "end"),
                    ("pool", "nrm", [("dve", "rec", 0)], lambda e, i, j: e.tensor_tensor(
                        side[:, bass.ds(i - 3, 4), :], side[:, bass.ds(i - 3, 4), :], rbuf[:], ALU.mult), "end"),
                ]
            prog.append(("act", "evac", [("dve", "c4", 2), ("out", 0)], lambda e, i, j: e.activation(
                pair(cin[:, j % 2, 2:2 + T1]), ps[:, 2 * (j % 2):2 * (j % 2) + 2, 0:HALF], ACT.Copy)))

            def tap(t):
                if t == 0:
                    return ("dve", "c0", [("act", "evac", 0), ("act", "silu", 2)], lambda e, i, j: e.tensor_scalar(
                        cacc[:, j % 2, :], cin[:, j % 2, 0:T1], pcol(cw, i), None, ALU.mult))
                return ("dve", f"c{t}", [("dve", f"c{t - 1}", 0)], lambda e, i, j: e.scalar_tensor_tensor(
                    cacc[:, j % 2, :], cin[:, j % 2, t:t + T1], pcol(cw, i, t), cacc[:, j % 2, :], ALU.mult, ALU.add))
            prog += [tap(t) for t in range(5)]
            prog.append(("act", "silu", [("dve", "c4", 0)], lambda e, i, j: e.activation(dst[:, i, :], cacc[:, j % 2, :], ACT.Silu), 1))
            return Linear(name, before, H // 4, 4, [(0, h_hi, h_lo, K8, True, True)],
                          lambda j, o: [ps[:, 2 * (j % 2) + v, 0:HALF] for v in range(2)],
                          {0: ("act", "evac", 2)}, prog, width=two)

        SERIES = 9

        def log1p_steps(tag):
            return [(tag, n) for n in ["den", "rec", "z", "z2", "a0"] + list(range(1, SERIES - 1)) + ["end"]]

        def log1p(e, st_, tag, y, t1, t2):
            names = log1p_steps(tag)
            c = [2.0 / (2 * k + 1) for k in range(SERIES)]
            todo = [lambda: e.tensor_scalar(t1, y, 2.0, None, ALU.add),
                    lambda: e.reciprocal(t2, t1),
                    lambda: e.tensor_tensor(y, y, t2, ALU.mult),
                    lambda: e.tensor_tensor(t1, y, y, ALU.mult),
                    lambda: e.tensor_scalar(t2, t1, c[SERIES - 1], None, ALU.mult)]
            for k in range(SERIES - 2, 0, -1):
                todo.append(lambda k=k: e.scalar_tensor_tensor(t2, t2, c[k], t1, ALU.add, ALU.mult))
            todo.append(lambda: e.scalar_tensor_tensor(y, t2, c[0], y, ALU.add, ALU.mult))
            for f, name in zip(todo, names):
                st_.did("dve", f(), name)
                st_.on(e, "dve", 0, name)

        class Gates(Stage):

            def __init__(self, before, pro):
                super().__init__("gates", before)
                self.pro = pro
                self.steps("pe", ["ba", "cum", "tail", "tot"])
                self.steps("dve", ["b", "a", "neg", "abs"] + log1p_steps("l") + ["sp", "g"])
                self.steps("act", ["sig", "eA", "ex", "ecol", "kcol", "lcol"])

            def pe(self, e):
                self.begin(e, "pe")
                self.pro.wait_whole(e, ("dve",))
                for c in range(NB):
                    t0 = META + (c - 1) * CH if c else 0
                    for k in range(KT):
                        for p3, (l, r) in enumerate(((h_hi, wba_hi), (h_lo, wba_hi), (h_hi, wba_lo))):
                            m = e.matmul(ps[:, 6, 32 * c:32 * c + 32], l[:, k, t0:t0 + P], r[:, k, :],
                                         start=(k == 0 and p3 == 0), stop=(k == KT - 1 and p3 == 2))
                self.did("pe", m, "ba")
                self.on(e, "dve", 0, "g")
                for step, mats, bank in (("cum", ("uf", "ub"), 5), ("tail", ("vf", "vb"), 7), ("tot", ("ones", "ones"), 4)):
                    for c in range(NB):
                        n = P if c else META
                        for d in range(2):
                            col = c * 2 * H + d * H
                            m = e.matmul(ps[:, bank, col:col + H], cmat(mats[d])[0:n, :], gdec[0:n, c, d * H:(d + 1) * H], start=True, stop=True)
                    self.did("pe", m, step)

            def dve(self, e):
                self.begin(e, "dve")
                ba = ps[:, 6, 0:32 * NB].rearrange("p (c n) -> p c n", c=NB)
                t = [tmpc[:, i, :] for i in range(4)]
                t0 = t[0].rearrange("p (c n) -> p c n", c=NB)
                dt = small[:, 16:32].unsqueeze(1).to_broadcast([P, NB, 16])
                ea = small[:, 32:48].unsqueeze(1).to_broadcast([P, NB, 16])
                self.on(e, "pe", 0, "ba")
                self.did("dve", e.tensor_copy(beta[:], ba[:, :, 0:16]), "b")
                self.did("dve", e.tensor_tensor(t0, ba[:, :, 16:32], dt, ALU.add), "a")
                self.on(e, "dve", 0, "a")
                self.did("dve", e.tensor_scalar(t[1], t[0], -1.0, None, ALU.mult), "neg")
                self.on(e, "dve", 0, "neg")
                self.did("dve", e.tensor_tensor(t[1], t[1], t[0], ALU.min), "abs")
                self.on(e, "act", 0, "ex")
                log1p(e, self, "l", t[1], t[2], t[3])
                self.did("dve", e.scalar_tensor_tensor(t[0], t[0], 0.0, t[1], ALU.max, ALU.add), "sp")
                self.on(e, "dve", 0, "sp")
                self.on(e, "act", 0, "eA")
                self.did("dve", e.scalar_tensor_tensor(gdec[:], t0, -1.0, ea, ALU.mult, ALU.mult), "g")

            def act(self, e):
                self.begin(e, "act")
                self.on(e, "dve", 0, "b")
                self.did("act", e.activation(beta[:], beta[:], ACT.Sigmoid), "sig")
                self.did("act", e.activation(small[:, 32:48], small[:, 0:16], ACT.Exp), "eA")
                self.on(e, "dve", 0, "abs")
                self.did("act", e.activation(tmpc[:, 1, :], tmpc[:, 1, :], ACT.Exp), "ex")
                for step, bank, name, dst in (("cum", 5, "ecol", ecol), ("tail", 7, "kcol", kcol), ("tot", 4, "lcol", lcol)):
                    self.on(e, "pe", 0, step)
                    self.did("act", e.activation(dst[:], ps[:, bank, 0:2 * H * NB].rearrange("p (c n) -> p c n", c=NB), ACT.Exp), name)

        class Turn(Stage):

            def __init__(self, before):
                super().__init__("turn", before)
                self.hb = [(t, h) for h in range(H) for t in "kv"]
                self.steps("pe", [("t", i) for i in range(2 * H)])
                self.steps("act", [("m", i) for i in range(2 * H)])
                self.steps("dve", [("c", i) for i in range(2 * H)])
                self.steps("pool", ["o0", "s0"])

            def pe(self, e):
                self.begin(e, "pe")
                for i, (t, h) in enumerate(self.hb):
                    src = kT if t == "k" else vT
                    b = 2 * (i % 4)
                    if i > 3:
                        self.on(e, "act", 0, ("m", i - 4))
                        self.on(e, "dve", 0, ("c", i - 4))
                    for c in range(NCH):
                        e.transpose(ps[:, b, c * P:(c + 1) * P], src[:, h, META + c * CH:META + (c + 1) * CH], cmat("ident"))
                    m = e.transpose(ps[0:META, b + 1, 0:P], src[:, h, 0:META], cmat("ident"))
                    self.did("pe", m, ("t", i))

            def dve(self, e):
                self.begin(e, "dve")
                for i, (t, h) in enumerate(self.hb):
                    self.on(e, "pe", 0, ("t", i))
                    dst = k_tok if t == "k" else v_tok
                    self.did("dve", e.tensor_copy(dst[:, :, h, :], ps[:, 2 * (i % 4), :].rearrange("p (c n) -> p c n", c=NCH)), ("c", i))

            def act(self, e):
                self.begin(e, "act")
                for i, (t, h) in enumerate(self.hb):
                    self.on(e, "pe", 0, ("t", i))
                    dst = k_met if t == "k" else v_met
                    self.did("act", e.activation(dst[0:META, h, :], ps[0:META, 2 * (i % 4) + 1, 0:P], ACT.Copy), ("m", i))

            def pool(self, e):
                self.begin(e, "pool")
                self.did("pool", e.memset(oT[:], 0.0), "o0")
                self.did("pool", e.memset(st[:, 1], 0.0), "s0")

        class Delta(Stage):

            def __init__(self, name, before, meta):
                super().__init__(name, before)
                self.meta = meta
                self.n = META if meta else CH
                self.levels = [b for b in LEVELS[1:] if b < self.n]
                self.pairs = [[(0, 0), (0, 1)]] if meta else [[(0, 0), (1, 0)], [(0, 1), (1, 1)]]
                L = self.levels
                lev = {"pe": [], "act": [], "dve": [], "pool": []}
                for b in L:
                    lev["pool"] += [f"e{b}"]
                    lev["pe"] += [f"tt{b}", f"xd{b}"]
                    lev["act"] += [f"tt{b}"]
                    lev["dve"] += [f"x{b}"] + ([f"xt{b}"] if b != L[-1] else [])
                ph = {
                    "pool": ["gv", "ab", "e1", "x1"] + (["ke"] if not meta else []) + lev["pool"] + ["kd"] + (["qd", "sl"] if not meta else []),
                    "act": ["gc", "kc", "dec"] + (["eg"] if not meta else []) + ["xt1"] + lev["act"],
                    "pe": ["kk", "dec", "xt1"] + lev["pe"] + (["ks"] if not meta else []) + ["w", "ds"] + (["o"] if not meta else []),
                    "dve": ["a"] + (["qk"] if not meta else []) + lev["dve"] + (["r"] if not meta else []) + ["vn", "s"] + (["o"] if not meta else []),
                }
                self.ph = ph
                for eng, names in ph.items():
                    self.steps(eng, [(x_, g, s) for g in range(len(self.pairs)) for x_ in names for s in range(2)], 1 if meta else NCH)

            def each(self, e, eng, fns):
                self.begin(e, eng)

                def body(it):
                    for g, pr in enumerate(self.pairs):
                        for name in self.ph[eng]:
                            for s, (d, half) in enumerate(pr):
                                self.asked = {}
                                self.did(eng, fns(name, it, g, s, d, half), (name, g, s))
                loop(e, 1 if self.meta else NCH, body)

            def w(self, e, it, g, s, eng, name, before=False):
                if not before:
                    self.ask(e, it, eng, (name, g, s), 0)
                elif g:
                    self.ask(e, it, eng, (name, g - 1, s), 0)
                else:
                    self.ask(e, it, eng, (name, len(self.pairs) - 1, s), 1)

            def ask(self, e, it, eng, step, back):
                n = self.log[eng].count(0, step, back)
                if n > self.asked.get(eng, (0,))[0]:
                    self.asked[eng] = (n, step, back)

            def flush(self, e, it):
                for eng, (_, step, back) in self.asked.items():
                    self.on(e, eng, it, step, back)
                self.asked = {}

            def chunk(self, it, d):
                if self.meta:
                    return 0, 0
                c = it if d == 0 else it * -1 + (NCH - 1)
                return c + 1, c

            def wt(self, name, s, n=None):
                n = n or self.n
                return work[name][0:n, s, :, 0:self.n]

            def bank(self, s, b, rows, cols):
                return ps[0:rows, 4 * s + b, 0:HG * cols].rearrange("p (u m) -> p u m", u=HG)

            def toks(self, t, it, d, half):
                if self.meta:
                    return t[:, half * HG:(half + 1) * HG, 0:META]
                c = self.chunk(it, d)[1]
                return t[:, half * HG:(half + 1) * HG, bass.ds(c * CH + META, CH)]

            def col(self, tab, it, d, half, width, rows=None):
                c = self.chunk(it, d)[0]
                h0 = d * H + half * HG
                return tab[0:(rows or self.n), c, h0:h0 + HG].unsqueeze(2).to_broadcast([rows or self.n, HG, width])

            def act(self, e):
                n = self.n

                def f(name, it, g, s, d, half):
                    w = lambda *q: self.w(e, it, g, s, *q)
                    if name == "gc":
                        w("pe", "dec", True)
                        c = self.chunk(it, d)[0]
                        self.flush(e, it)
                        return e.activation(small[0:n, 112 + HG * s:112 + HG * s + HG], gdec[0:n, c, d * H + half * HG:d * H + half * HG + HG], ACT.Copy)
                    if name == "kc":
                        w("pe", "kk", True)
                        if not self.meta:
                            w("pe", "ks", True)
                            w("pool", "ke", True)
                        self.flush(e, it)
                        return e.activation(work["kc"][:, s, :, 0:n], self.toks(kT, it, d, half), ACT.Copy)
                    if name == "dec":
                        w("pe", "dec")
                        if not self.meta:
                            w("pe", "o", True)
                        else:
                            w("dve", "a", True)
                        self.flush(e, it)
                        return e.activation(self.wt("dec", s), self.bank(s, 0, n, n), ACT.Exp)
                    if name == "eg":
                        w("pool", "qd", True)
                        self.flush(e, it)
                        return e.activation(work["eg"][:, s, :, :], self.bank(s, 1, P, n), ACT.Exp)
                    if name == "xt1":
                        w("pe", "xt1")
                        if not self.meta:
                            w("pe", "o", True)
                        self.flush(e, it)
                        return e.activation(self.wt("xt", s), self.bank(s, 0, n, n), ACT.Copy)
                    w("pe", name)
                    self.flush(e, it)
                    return e.activation(self.wt("tt", s), self.bank(s, 1, n, n), ACT.Copy)
                self.each(e, "act", f)

            def pool(self, e):
                n = self.n

                def f(name, it, g, s, d, half):
                    w = lambda *q: self.w(e, it, g, s, *q)
                    A, E = self.wt("a", s), self.wt("e", s)
                    if name == "gv":
                        w("act", "gc")
                        w("pe", "w", True)
                        gb = small[0:n, 112 + HG * s:112 + HG * s + HG].unsqueeze(2).to_broadcast([n, HG, n])
                        v = cmat("vb" if d else "vf")[0:n, 0:n].unsqueeze(1).to_broadcast([n, HG, n])
                        self.flush(e, it)
                        return e.tensor_tensor(E, v, gb, ALU.mult)
                    if name == "ab":
                        w("dve", "a")
                        self.flush(e, it)
                        return e.tensor_tensor(A, A, self.col(beta, it, d, half, n), ALU.mult)
                    if name[0] == "e":
                        if name == "e1":
                            w("pool", "ab")
                            w("pe", "dec")
                        else:
                            b = int(name[1:])
                            w("pe", f"tt{b // 2}") if b > 2 else w("pool", "x1")
                        m = cmat("m" + name[1:])[0:n, 0:n].unsqueeze(1).to_broadcast([n, HG, n])
                        self.flush(e, it)
                        return e.tensor_tensor(E, A, m, ALU.mult)
                    if name == "x1":
                        w("pool", "e1")
                        w("pe", "w", True)
                        i = cmat("ident")[0:n, 0:n].unsqueeze(1).to_broadcast([n, HG, n])
                        self.flush(e, it)
                        return e.tensor_tensor(self.wt("x", s), i, E, ALU.subtract)
                    if name == "ke":
                        w("act", "eg")
                        w("pe", "kk")
                        self.flush(e, it)
                        return e.tensor_tensor(work["kc"][:, s], work["kc"][:, s], work["eg"][:, s], ALU.mult)
                    if name == "kd":
                        w("pool", f"e{self.levels[-1]}")
                        kt = k_met[0:n, half * HG:(half + 1) * HG, :] if self.meta else k_tok[:, self.chunk(it, d)[1], half * HG:(half + 1) * HG, :]
                        self.flush(e, it)
                        return e.tensor_tensor(work["a"][0:n, s], kt, self.col(kcol, it, d, half, P), ALU.mult)
                    if name == "qd":
                        w("pe", f"tt{self.levels[-1]}")
                        self.flush(e, it)
                        return e.tensor_tensor(work["xt"][:, s], self.toks(qT, it, d, half), work["eg"][:, s], ALU.mult)
                    if name == "sl":
                        w("pool", "qd")
                        self.on_state(e, it, g, s)
                        S = st[:, d, half * HG:(half + 1) * HG, :]
                        self.flush(e, it)
                        return e.tensor_tensor(work["eg"][:, s], S, self.col(lcol, it, d, half, P, P), ALU.mult)
                self.each(e, "pool", f)

            def pe(self, e):
                n = self.n
                I4 = range(HG)

                def f(name, it, g, s, d, half):
                    w = lambda *q: self.w(e, it, g, s, *q)
                    bk = lambda b, rows, cols: self.bank(s, b, rows, cols)
                    E, X, XT, TT = self.wt("e", s), self.wt("x", s), self.wt("xt", s), self.wt("tt", s)
                    S = st[:, d, half * HG:(half + 1) * HG, :]
                    kc = work["kc"]
                    if name == "kk":
                        w("act", "kc")
                        w("dve", "s", True)
                        if not self.meta:
                            w("dve", "o", True)
                        self.flush(e, it)
                        for u in I4:
                            m = e.matmul(bk(2, n, n)[:, u], kc[:, s, u, 0:n], kc[:, s, u, 0:n], start=True, stop=True)
                            if not self.meta:
                                c = self.chunk(it, d)[1]
                                m = e.matmul(bk(3, n, n)[:, u], kc[:, s, u, 0:n], qT[:, half * HG + u, bass.ds(c * CH + META, CH)], start=True, stop=True)
                        return m
                    if name == "dec":
                        w("pool", "gv")
                        if not self.meta:
                            w("dve", "r", True)
                        w("dve", "vn", True)
                        U = cmat("ub" if d else "uf")
                        self.flush(e, it)
                        for u in I4:
                            e.matmul(bk(0, n, n)[:, u], E[:, u], U[0:n, 0:n], start=True, stop=False)
                            m = e.matmul(bk(0, n, n)[:, u], cb[0:n, 0, 0:n], cb[0:n, 1 + d, 0:n], start=False, stop=True)
                        if not self.meta:
                            self.flush(e, it)
                            for u in I4:
                                gcol = small[:, 112 + HG * s + u:113 + HG * s + u].to_broadcast([P, P])
                                m = e.matmul(bk(1, P, n)[:, u], gcol, U, start=True, stop=True)
                        return m
                    if name == "xt1":
                        w("pool", "x1")
                        w("act", "dec")
                        self.flush(e, it)
                        for u in I4:
                            m = e.transpose(bk(0, n, n)[:, u], X[:, u], cmat("ident")[0:n, 0:n])
                        return m
                    if name[:2] == "tt":
                        b = int(name[2:])
                        w("pool", f"e{b}")
                        if b == 2:
                            w("act", "xt1")
                            if not self.meta:
                                w("act", "eg")
                        else:
                            w("dve", f"xt{b // 2}")
                            w("act", f"tt{b // 2}")
                        self.flush(e, it)
                        for u in I4:
                            m = e.matmul(bk(1, n, n)[:, u], E[:, u], XT[:, u], start=True, stop=True)
                        return m
                    if name[:2] == "xd":
                        b = int(name[2:])
                        w("act", f"tt{b}")
                        if b == 2:
                            w("dve", "a" if self.meta else "qk")
                        self.flush(e, it)
                        for u in I4:
                            m = e.matmul(bk(2, n, n)[:, u], TT[:, u], X[:, u], start=True, stop=True)
                        if b != self.levels[-1]:
                            self.flush(e, it)
                            for u in I4:
                                m = e.matmul(bk(3, n, n)[:, u], X[:, u], TT[:, u], start=True, stop=True)
                        return m
                    if name == "ks":
                        w("pool", "ke")
                        w("act", "xt1")
                        self.on_state(e, it, g, s)
                        self.flush(e, it)
                        for u in I4:
                            m = e.matmul(bk(0, n, P)[:, u], kc[:, s, u, :], S[:, u], start=True, stop=True)
                        return m
                    if name == "w":
                        w("dve", f"x{self.levels[-1]}")
                        w("act", f"tt{self.levels[-1]}")
                        if not self.meta:
                            w("dve", "r")
                        self.flush(e, it)
                        for u in I4:
                            r = v_met[0:n, half * HG + u, :] if self.meta else work["e"][:, s, u, :]
                            m = e.matmul(bk(1, n, P)[:, u], X[:, u], r, start=True, stop=True)
                        return m
                    if name == "ds":
                        w("pool", "kd")
                        w("dve", "vn")
                        self.flush(e, it)
                        for u in I4:
                            m = e.matmul(bk(3, P, P)[:, u], work["a"][0:n, s, u, :], work["tt"][0:n, s, u, :], start=True, stop=True)
                        return m
                    if name == "o":
                        w("pool", "qd")
                        self.flush(e, it)
                        for u in I4:
                            e.matmul(bk(2, P, n)[:, u], S[:, u], work["xt"][:, s, u, :], start=True, stop=False)
                            m = e.matmul(bk(2, P, n)[:, u], work["tt"][:, s, u, :], work["dec"][:, s, u, :], start=False, stop=True)
                        return m
                self.each(e, "pe", f)

            def on_state(self, e, it, g, s):
                self.ask(e, it, "dve", ("s", g, s), 1)

            def dve(self, e):
                n = self.n

                def f(name, it, g, s, d, half):
                    w = lambda *q: self.w(e, it, g, s, *q)
                    bk = lambda b, rows, cols: self.bank(s, b, rows, cols)
                    X, XT = self.wt("x", s), self.wt("xt", s)
                    S = st[:, d, half * HG:(half + 1) * HG, :]
                    if name == "a":
                        w("pe", "kk")
                        w("act", "dec")
                        w("pe", "ds", True)
                        self.flush(e, it)
                        return e.tensor_tensor(self.wt("a", s), bk(2, n, n), self.wt("dec", s), ALU.mult)
                    if name == "qk":
                        w("dve", "a")
                        self.flush(e, it)
                        return e.tensor_tensor(self.wt("dec", s), bk(3, n, n), self.wt("dec", s), ALU.mult)
                    if name == "r":
                        w("pe", "ks")
                        w("pe", f"tt{self.levels[-1]}")
                        v = v_tok[:, self.chunk(it, d)[1], half * HG:(half + 1) * HG, :]
                        self.flush(e, it)
                        return e.tensor_tensor(work["e"][:, s], v, bk(0, n, P), ALU.subtract)
                    if name == "vn":
                        w("pe", "w")
                        w("pe", f"xd{self.levels[-1]}")
                        self.flush(e, it)
                        return e.tensor_tensor(work["tt"][0:n, s], bk(1, n, P), self.col(beta, it, d, half, P), ALU.mult)
                    if name == "s":
                        w("pe", "ds")
                        if self.meta:
                            self.flush(e, it)
                            return e.tensor_copy(S, bk(3, P, P))
                        w("pool", "sl")
                        w("pe", "o")
                        self.flush(e, it)
                        return e.tensor_tensor(S, work["eg"][:, s], bk(3, P, P), ALU.add)
                    if name == "o":
                        w("pe", "o")
                        w("dve", "o", True)
                        o = oT[:, half * HG:(half + 1) * HG, bass.ds(self.chunk(it, d)[1] * CH, CH)]
                        self.flush(e, it)
                        return e.tensor_tensor(o, o, bk(2, P, n), ALU.add)
                    if name[:2] == "xt":
                        b = int(name[2:])
                        w("pe", f"xd{b}")
                        w("act", "xt1") if b == 2 else w("dve", f"xt{b // 2}")
                        self.flush(e, it)
                        return e.tensor_tensor(XT, XT, bk(3, n, n), ALU.subtract)
                    b = int(name[1:])
                    w("pe", f"xd{b}")
                    self.flush(e, it)
                    return e.tensor_tensor(X, X, bk(2, n, n), ALU.subtract)
                self.each(e, "dve", f)

        def row(i, n=SEQ, off=0):
            return tmp[:, i, off:off + n]

        zeroed = [0]

        def zero(e, *aps):
            for ap in aps:
                e.memset(ap, 0.0).then_inc(s_zero, 1)
            zeroed[0] += len(aps)
            e.wait_ge(s_zero, zeroed[0])

        TOK = ((META, T1),)
        ALL = ((0, SEQ),)

        def split(dst_hi, dst_lo, val, done, tile=lambda i: i):
            return [("act", "hi", [("dve", done, 0)], lambda e, i, j: e.activation(dst_hi[:, tile(i), :], row(val + j % 2), ACT.Copy), 1),
                    ("pool", "lo", [("act", "hi", 0)], lambda e, i, j: e.tensor_tensor(
                        dst_lo[:, tile(i), :], row(val + j % 2), dst_hi[:, tile(i), :].bitcast(F32), ALU.subtract), 1)]

        def one(b0):
            return lambda j, o: [ps[:, b0 + j % 4, :]]

        def gate_z(before):
            tail = []
            for j in range(4):
                g = lambda i, j=j: i - 3 + j
                tail += [
                    ("dve", f"n{j}", [("dve", "rec", 0)], lambda e, i, _, j=j, g=g: e.scalar_tensor_tensor(
                        oT[:, g(i), :], oT[:, g(i), :], pcol("dnn", 0), row(4 + j), ALU.mult, ALU.mult), "end"),
                    ("dve", f"v{j}", [("dve", f"n{j}", 0), ("act", "silu", 3 - j)], lambda e, i, _, g=g: e.tensor_tensor(
                        zs[:, g(i), :], zs[:, g(i), :], oT[:, g(i), :], ALU.mult), "end"),
                    ("act", f"hi{j}", [("dve", f"v{j}", 0)], lambda e, i, _, g=g: e.activation(od_hi[:, g(i), :], zs[:, g(i), :], ACT.Copy), "end"),
                    ("pool", f"lo{j}", [("act", f"hi{j}", 0)], lambda e, i, _, g=g: e.tensor_tensor(
                        od_lo[:, g(i), :], zs[:, g(i), :], od_hi[:, g(i), :].bitcast(F32), ALU.subtract), "end"),
                ]
            r4 = tmp[:, 4:8, 0:SEQ]
            return Linear("z", before, H // 4, 4, [(0, h_hi, h_lo, K8, True, True)], one(0), {0: ("act", "silu", 4)}, [
                ("act", "presq", [("pe", "ss", 2)], lambda e, i, j: e.activation(row(j % 2), oT[:, i, :], ACT.Square)),
                ("pe", "ss", [("act", "presq", 0), ("act", "rc", 1)], lambda e, i, j: e.matmul(ps[:, 4, :], cmat("mean128"), row(j % 2), start=True, stop=True)),
                ("act", "silu", [("out", 0)], lambda e, i, j: e.activation(zs[:, i, :], ps[:, j % 4, :], ACT.Silu)),
                ("act", "rc", [("pe", "ss", 0), ("dve", "v3", "end")], lambda e, i, j: e.activation(row(4 + j), ps[:, 4, :], ACT.Copy), 1),
                ("act", "rt", [("act", "rc", 0)], lambda e, i, j: e.activation(r4, r4, ACT.Sqrt, bias=eps_col), "end"),
                ("dve", "rec", [("act", "rt", 0)], lambda e, i, j: e.reciprocal(r4, r4), "end"),
            ] + tail, width=TOK)

        CW = SEQ + 4
        def short_conv(before):
            wide = ((META - 4, META - 4 + CW // 2), (META - 4 + CW // 2, T1))
            bank = lambda j, o: ([ps[:, 2 * o, 0:CW // 2], ps[:, 2 * o + 1, 0:CW // 2]] if o < 2 else [ps[:, 4 + j % 2, :]])

            def tap(t):
                if t == 0:
                    return ("dve", "c0", [("dve", "cx", 0), ("pool", "lo", 2)], lambda e, i, j: e.tensor_scalar(
                        row(4 + j % 2), row(1, SEQ, 3), pcol("sc", i), None, ALU.mult))
                return ("dve", f"c{t}", [("dve", f"c{t - 1}", 0)], lambda e, i, j: e.scalar_tensor_tensor(
                    row(4 + j % 2), row(1, SEQ, 3 + t), pcol("sc", i, t), row(4 + j % 2), ALU.mult, ALU.add))
            return Linear("sc", before, KT // 4, 4, [(o, h_hi, h_lo, K8, True, True) for o in range(3)], bank,
                          {0: ("act", "c", 1), 1: ("dve", "cx", 1), 2: ("dve", "v", 2)}, [
                ("act", "c", [("out", 0), ("dve", "cx", 1)], lambda e, i, j: e.activation(pair(row(0, CW)), ps[:, 0:2, 0:CW // 2], ACT.Copy)),
                ("dve", "cx", [("out", 1), ("act", "c", 0), ("dve", "c2", 1)], lambda e, i, j: e.tensor_tensor(
                    pair(row(1, CW)), ps[:, 2:4, 0:CW // 2], pair(row(0, CW)), ALU.mult)),
                tap(0), tap(1), tap(2),
                ("dve", "v", [("out", 2), ("dve", "c2", 0)], lambda e, i, j: e.tensor_tensor(row(4 + j % 2), row(4 + j % 2), ps[:, 4 + j % 2, :], ALU.mult)),
            ] + split(sc_hi, sc_lo, 4, "v"), width={0: wide, 1: wide, 2: TOK},
                start={"dve": lambda e: zero(e, row(1, 4, CW))})

        def two_banks(j, o):
            return [ps[:, 2 * (j % 2) + o, :]]

        def branch_sc(before):
            return Linear("bsc", before, KT // 2, 2, [(0, h_hi, h_lo, K8, True, True), (1, sc_hi, sc_lo, K8, True, True)], two_banks,
                          {0: ("act", "sg", 2), 1: ("dve", "v", 2)}, [
                ("act", "sg", [("out", 0), ("dve", "v", 2)], lambda e, i, j: e.activation(row(j % 2), ps[:, 2 * (j % 2), :], ACT.Sigmoid)),
                ("dve", "v", [("out", 1), ("act", "sg", 0)], lambda e, i, j: e.tensor_tensor(m1[:, i, :], row(j % 2), ps[:, 2 * (j % 2) + 1, :], ALU.mult)),
            ], width={0: TOK, 1: ALL})

        def branch_dn(before):
            return Linear("bdn", before, KT // 2, 2, [(0, h_hi, h_lo, K8, True, True), (1, od_hi, od_lo, K8, True, True)], two_banks,
                          {0: ("act", "sg", 2), 1: ("dve", "t", 2)}, [
                ("act", "sg", [("out", 0), ("dve", "t", 2)], lambda e, i, j: e.activation(row(j % 2), ps[:, 2 * (j % 2), :], ACT.Sigmoid)),
                ("dve", "t", [("out", 1), ("act", "sg", 0), ("pool", "lo", 2)], lambda e, i, j: e.tensor_tensor(
                    row(2 + j % 2), row(j % 2), ps[:, 2 * (j % 2) + 1, :], ALU.mult)),
                ("dve", "v", [("dve", "t", 0)], lambda e, i, j: e.tensor_tensor(row(2 + j % 2), row(2 + j % 2), m1[:, i, :], ALU.add)),
            ] + split(me_hi, me_lo, 2, "v"), width={0: TOK, 1: ALL},
                start={"act": lambda e: e.dma_start(x_res[:], a["x"][:, :, META:T1]).then_inc(s_xr, 16)})

        def residual(name, before, hi, lo, parts, first=None, final=False):
            n = len(parts)
            m = 4 if n != 2 else 2
            units, k = [], 0
            for p_, c in enumerate(parts):
                units.append((0, hi, lo, [(t, k + t) for t in range(c)], p_ == 0, p_ == n - 1))
                k += c
            src = x if first is None else first
            return Linear(name, before, KT // m, m, units, one(0), {0: ("dve", "v", min(m, 4))}, [
                ("dve", "v", [("out", 0)], lambda e, i, j: e.tensor_tensor(x[:, i, :], src[:, i, :], ps[:, j % 4, :], ALU.add)),
            ], width=ALL, final=final, start={"dve": lambda e: e.wait_ge(s_xr, 16)})

        def gate_up(before):
            return Linear("gu", before, FT // 2, 2, [(0, h_hi, h_lo, K8, True, True), (1, h_hi, h_lo, K8, True, True)], two_banks,
                          {0: ("act", "sg", 2), 1: ("dve", "v", 2)}, [
                ("act", "sg", [("out", 0), ("dve", "v", 2)], lambda e, i, j: e.activation(row(j % 2), ps[:, 2 * (j % 2), :], ACT.Silu)),
                ("dve", "v", [("out", 1), ("act", "sg", 0), ("pool", "lo", 2)], lambda e, i, j: e.tensor_tensor(
                    row(2 + j % 2), row(j % 2), ps[:, 2 * (j % 2) + 1, :], ALU.mult)),
            ] + split(y_hi, y_lo, 2, "v"), width=TOK)

        def glu_conv(before):
            taps = PAR["ca"][2]

            def tap(t):
                if t == 0:
                    return ("dve", "c0", [("dve", "u", 0)], lambda e, i, j: e.tensor_scalar(
                        uc[:, i, :], row(2), pcol("ca", i), pcol("cab", i), ALU.mult, ALU.add))
                return ("dve", f"c{t}", [("dve", f"c{t - 1}", 0)], lambda e, i, j: e.scalar_tensor_tensor(
                    uc[:, i, :], row(2, SEQ, t), pcol("ca", i, t), uc[:, i, :], ALU.mult, ALU.add))
            return Linear("glu", before, KT // 2, 2, [(0, h_hi, h_lo, K8, True, True), (1, h_hi, h_lo, K8, True, True)], two_banks,
                          {0: ("dve", "u", 2), 1: ("act", "sg", 2)}, [
                ("act", "sg", [("out", 1), ("dve", "u", 2)], lambda e, i, j: e.activation(row(j % 2), ps[:, 2 * (j % 2) + 1, :], ACT.Sigmoid)),
                ("dve", "u", [("out", 0), ("act", "sg", 0), ("dve", f"c{taps - 1}", 1)], lambda e, i, j: e.tensor_tensor(
                    row(2, SEQ, taps - 1), row(j % 2), ps[:, 2 * (j % 2), :], ALU.mult)),
            ] + [tap(t) for t in range(taps)], width=TOK,
                start={"dve": lambda e: zero(e, row(2, taps - 1))})

        class PoolDiff(Linear):

            def __init__(self, before):
                self.off = 16
                prog = [("act", "bv", [("out", 0), ("pool", "lo", 2)], lambda e, i, j: e.activation(row(j % 2, SEQ, 16), ps[:, j % 4, :], ACT.Copy))]
                for j in range(KT):
                    pass
                super().__init__("bval", before, 1, KT, [(0, h_hi, h_lo, K8, True, True)], one(0), {0: ("act", "bv", 4)}, [], width=TOK)
                names = []
                for j in range(KT):
                    names += [("s", j, n) for n in range(j // 2 + 1)] + [("d", j), ("q", j), ("f", j)]
                self.steps("dve", names)
                self.steps("pool", [("lo", j) for j in range(KT)])
                self.steps("act", [(n_, j) for j in range(KT) for n_ in ("bv", "hi")])

            def act(self, e):
                self.begin(e, "act")
                for j in range(KT):
                    c = j + 2
                    round_unit(e, BASE["bval"] + c, c)
                    e.wait_ge(s_pe, BASE["bval"] + j + 1)
                    if j > 1:
                        self.on(e, "dve", 0, ("f", j - 2))
                    self.did("act", e.activation(row(j % 2, SEQ, 16), ps[:, j % 4, :], ACT.Copy), ("bv", j))
                    self.on(e, "dve", 0, ("f", j))
                    self.did("act", e.activation(mx_hi[:, j, :], row(4 + j % 2), ACT.Copy), ("hi", j))

            def pool(self, e):
                self.begin(e, "pool")
                for j in range(KT):
                    split_unit(e, BASE["bval"] + j + 2, j + 2)
                    self.on(e, "act", 0, ("hi", j))
                    self.did("pool", e.tensor_tensor(mx_lo[:, j, :], row(4 + j % 2), mx_hi[:, j, :].bitcast(F32), ALU.subtract), ("lo", j))

            def dve(self, e):
                self.begin(e, "dve")
                zero(e, *[row(r, 16) for r in range(4)])
                for j in range(KT):
                    w = POOLW[j // 2]
                    self.on(e, "act", 0, ("bv", j))
                    last = ("f", j - 1)
                    src = j % 2
                    for n in range(j // 2 + 1):
                        if last[1] >= 0:
                            self.on(e, "dve", 0, last)
                        dst = 2 + n % 2
                        self.did("dve", e.tensor_tensor(row(dst, SEQ, 16), row(src, SEQ, 16), row(src, SEQ, 16 - 2 ** n), ALU.add), ("s", j, n))
                        last, src = ("s", j, n), dst
                    self.on(e, "dve", 0, last)
                    if j > 1:
                        self.on(e, "pool", 0, ("lo", j - 2))
                    v = row(4 + j % 2)
                    self.did("dve", e.scalar_tensor_tensor(v, row(src, SEQ, 16), 1.0 / w, row(j % 2, SEQ, 16), ALU.mult, ALU.subtract), ("d", j))
                    cnt = small[:, 48 + 16 * (j // 2):64 + 16 * (j // 2)]
                    self.did("dve", e.tensor_tensor(row(6, 16), row(src, 16, 16), cnt, ALU.mult), ("q", j))
                    self.on(e, "dve", 0, ("q", j))
                    self.did("dve", e.tensor_tensor(v[:, 0:16], row(6, 16), row(j % 2, 16, 16), ALU.subtract), ("f", j))

        def pool_mix(before):
            def emit(o):
                return lambda e, i, j: e.tensor_scalar(yb[:, i * 2 + o, :], ps[:, 2 * (j % 2) + o, :], pcol("pb", i * 2 + o), pcol("psc", i * 2 + o), ALU.add, ALU.mult)
            tiles = [[(2 * o + k, lambda j, k=k: 2 * j + k) for k in range(2)] for o in range(2)]
            return Linear("pool", before, 1, 4, [(0, mx_hi, mx_lo, tiles, True, True)],
                          lambda j, o: [[ps[:, 2 * (j % 2), :]], [ps[:, 2 * (j % 2) + 1, :]]], {0: ("dve", "v1", 2)}, [
                ("dve", "v0", [("out", 0)], emit(0)),
                ("dve", "v1", [("out", 0)], emit(1)),
            ], width=ALL)

        def gated(name, before, val, hi, lo, n, tile=lambda i: i):
            return Linear(name, before, n // 4, 4, [(0, h_hi, h_lo, K8, True, True)], one(0), {0: ("act", "sg", 4)}, [
                ("act", "sg", [("out", 0), ("dve", "v", 2)], lambda e, i, j: e.activation(row(j % 2), ps[:, j % 4, :], ACT.Silu)),
                ("dve", "v", [("act", "sg", 0), ("pool", "lo", 2)], lambda e, i, j: e.tensor_tensor(row(2 + j % 2), row(j % 2), val[:, i, :], ALU.mult)),
            ] + split(hi, lo, 2, "v", tile), width=TOK)

        class LayerNorm(Stage):

            def __init__(self, before):
                super().__init__("ln", before)
                K = range(KT)
                self.steps("pe", ["mu"] + [("ss", k) for k in K])
                self.steps("act", [("sq", k) for k in K] + ["rt"] + [("u", k) for k in K])
                self.steps("dve", ["mu"] + [("c", k) for k in K] + ["r"] + [("n", k) for k in K])

            def pe(self, e):
                self.begin(e, "pe")
                for k in range(KT):
                    mm = e.matmul(ps[:, 4, :], cmat("mean1024"), uc[:, k, :], start=(k == 0), stop=(k == KT - 1))
                self.did("pe", mm, "mu")
                for k in range(KT):
                    self.on(e, "act", 0, ("sq", k))
                    self.did("pe", e.matmul(ps[:, 5, :], cmat("mean1024"), row(k % 2), start=(k == 0), stop=(k == KT - 1)), ("ss", k))

            def act(self, e):
                self.begin(e, "act")
                for k in range(KT):
                    self.on(e, "dve", 0, ("c", k))
                    if k > 1:
                        self.on(e, "pe", 0, ("ss", k - 2))
                    self.did("act", e.activation(row(k % 2), uc[:, k, :], ACT.Square), ("sq", k))
                self.on(e, "pe", 0, ("ss", KT - 1))
                self.did("act", e.activation(row(3), ps[:, 5, :], ACT.Sqrt, bias=small[:, 126:127]), "rt")
                for k in range(KT):
                    self.on(e, "dve", 0, ("n", k))
                    self.did("act", e.activation(uc[:, k, :], uc[:, k, :], ACT.Silu, bias=pcol("lnb", k), scale=pcol("lng", k)), ("u", k))

            def dve(self, e):
                self.begin(e, "dve")
                self.on(e, "pe", 0, "mu")
                self.did("dve", e.tensor_copy(row(2), ps[:, 4, :]), "mu")
                self.on(e, "dve", 0, "mu")
                for k in range(KT):
                    self.did("dve", e.tensor_tensor(uc[:, k, :], uc[:, k, :], row(2), ALU.subtract), ("c", k))
                self.on(e, "act", 0, "rt")
                self.did("dve", e.reciprocal(row(3), row(3)), "r")
                self.on(e, "dve", 0, "r")
                for k in range(KT):
                    self.did("dve", e.tensor_tensor(uc[:, k, :], uc[:, k, :], row(3), ALU.mult), ("n", k))

        def lru_conv(before):
            def tap(t):
                if t == 0:
                    return ("dve", "c0", [("act", "evac", 0)], lambda e, i, j: e.tensor_scalar(
                        xc[:, i, :], row(j % 2), pcol("cc", i), pcol("ccb", i), ALU.mult, ALU.add))
                return ("dve", f"c{t}", [("dve", f"c{t - 1}", 0)], lambda e, i, j: e.scalar_tensor_tensor(
                    xc[:, i, :], row(j % 2, SEQ, t), pcol("cc", i, t), xc[:, i, :], ALU.mult, ALU.add))
            return Linear("xr", before, LT // 4, 4, [(0, h_hi, h_lo, K8, True, True)], one(0), {0: ("act", "evac", 4)}, [
                ("act", "evac", [("out", 0), ("dve", "c3", 2)], lambda e, i, j: e.activation(row(j % 2, SEQ, 3), ps[:, j % 4, :], ACT.Copy)),
                tap(0), tap(1), tap(2), tap(3),
                ("act", "hi", [("dve", "c3", 0)], lambda e, i, j: e.activation(xc_hi[:, i, :], xc[:, i, :], ACT.Copy), 1),
                ("pool", "lo", [("act", "hi", 0)], lambda e, i, j: e.tensor_tensor(xc_lo[:, i, :], xc[:, i, :], xc_hi[:, i, :].bitcast(F32), ALU.subtract), 1),
            ], width=TOK, start={"dve": lambda e: zero(e, row(0, 3), row(1, 3))})

        rt_t = z("rt_t", [P, LT, SEQ], L24)
        lamc = small[:, 112:124]

        class Lambda(Stage):

            def __init__(self, before):
                super().__init__("lam", before)
                self.steps("act", ["ex"])
                self.steps("dve", ["x", "neg", "abs"] + log1p_steps("l") + ["sp", "c"])

            def act(self, e):
                self.begin(e, "act")
                self.on(e, "dve", 0, "abs")
                self.did("act", e.activation(row(1, LT), row(1, LT), ACT.Exp), "ex")

            def dve(self, e):
                self.begin(e, "dve")
                o = PAR["lam"][0]
                t = [row(r, LT) for r in range(4)]
                self.did("dve", e.tensor_scalar(t[0], par[:, o:o + LT], -1.0, None, ALU.mult), "x")
                self.on(e, "dve", 0, "x")
                self.did("dve", e.tensor_scalar(t[1], t[0], -1.0, None, ALU.mult), "neg")
                self.on(e, "dve", 0, "neg")
                self.did("dve", e.tensor_tensor(t[1], t[1], t[0], ALU.min), "abs")
                self.on(e, "act", 0, "ex")
                log1p(e, self, "l", t[1], t[2], t[3])
                self.did("dve", e.scalar_tensor_tensor(t[0], t[0], 0.0, t[1], ALU.max, ALU.add), "sp")
                self.on(e, "dve", 0, "sp")
                self.did("dve", e.tensor_scalar(lamc, t[0], -4.0, None, ALU.mult), "c")

        def lru(before):
            prog = []
            tiles = []
            for q in range(3):
                tiles += [[(2 * q, lambda j, q=q: 3 * j + q)], [(2 * q + 1, lambda j, q=q: 3 * j + q)]]
            for q in range(3):
                pv = 2 if q == 0 else q - 1
                bk = 1 if q == 0 else 0
                ch = lambda i, q=q: i * 3 + q
                prog += [
                    ("act", f"r{q}", [("out", 0), ("act", f"t{pv}", bk)], lambda e, i, j, q=q, ch=ch: e.activation(row(0), ps[:, 2 * q, :], ACT.Sigmoid, bias=pcol("brg", ch(i)))),
                    ("act", f"i{q}", [("dve", f"ix{pv}", bk)], lambda e, i, j, q=q, ch=ch: e.activation(row(1), ps[:, 2 * q + 1, :], ACT.Sigmoid, bias=pcol("big", ch(i)))),
                    ("act", f"t{q}", [("act", f"r{q}", 0)], lambda e, i, j, q=q, ch=ch: e.activation(hs[:, ch(i), :], row(0), ACT.Tanh, scale=lamc_col(ch(i)))),
                    ("dve", f"ix{q}", [("act", f"i{q}", 0)], lambda e, i, j, ch=ch: e.tensor_tensor(xc[:, ch(i), :], row(1), xc[:, ch(i), :], ALU.mult)),
                ]
            prog.append(("act", "rt", [("out", 0), ("act", "t2", 0)], lambda e, i, j: e.activation(rt_t[:], hs[:], ACT.Sqrt, scale=-1.0), "end"))
            return Linear("lru", before, 1, 4, [(0, xc_hi, xc_lo, tiles, True, True)],
                          lambda j, o: [[ps[:, b, :]] for b in range(6)], {0: ("act", "i2", 1)}, prog, width=ALL)

        def lru_scan(before):
            return Linear("lgate", before, LT // 4, 4, [(0, h_hi, h_lo, K8, True, True)], one(0), {0: ("act", "sg", 4)}, [
                ("act", "sg", [("out", 0), ("dve", "v", 2)], lambda e, i, j: e.activation(row(j % 2), ps[:, j % 4, :], ACT.Silu)),
                ("dve", "dn", [("dve", "q", 1)], lambda e, i, j: e.tensor_scalar(row(4), hs[:, i, :], -1.0, 1.0, ALU.mult, ALU.add)),
                ("dve", "q", [("dve", "dn", 0), ("dve", "b", 1)], lambda e, i, j: e.reciprocal(row(5), row(4))),
                ("dve", "a", [("dve", "q", 0), ("dve", "h", 1)], lambda e, i, j: e.scalar_tensor_tensor(row(6), hs[:, i, :], 1.0, row(5), ALU.add, ALU.mult)),
                ("dve", "b", [("dve", "h", 1)], lambda e, i, j: e.scalar_tensor_tensor(row(7), rt_t[:, i, :], 2.0, row(5), ALU.mult, ALU.mult)),
                ("dve", "bx", [("dve", "b", 0)], lambda e, i, j: e.tensor_tensor(row(7), row(7), xc[:, i, :], ALU.mult)),
                ("dve", "h", [("dve", "bx", 0)], lambda e, i, j: e.tensor_tensor_scan(hs[:, i, :], row(6), row(7), 0.0, ALU.mult, ALU.add)),
                ("dve", "v", [("act", "sg", 0), ("dve", "h", 0), ("pool", "lo", 2)], lambda e, i, j: e.tensor_tensor(row(2 + j % 2), row(j % 2), hs[:, i, :], ALU.mult)),
            ] + split(xc_hi, xc_lo, 2, "v"), width=TOK)

        def lamc_col(c):
            return small[:, 112:124].rearrange("p (n k) -> p n k", k=1)[:, c, :]

        class Output(Stage):
            def __init__(self, before):
                super().__init__("store", before)

            def sp(self, e):
                for k in range(0, KT, 2):
                    self.before.on(e, "dve", 0, ("h", k + 1))
                    e.dma_start(out[:, k:k + 2, :], x[:, k:k + 2, :]).then_inc(s_out, 16)
                e.wait_ge(s_out, 16 * KT // 2)

        pro = Prologue()
        n1 = Norm("norm1", pro, x_in, "norm1", T1, hf=hf0, sq=sqv, rr=rrow)
        q_ = qkv("q", n1, "cq", qT, None, None)
        k_ = qkv("k", q_, "ck", kT, qT, "ones128")
        v_ = qkv("v", k_, "cv", vT, kT, "ones")
        ga = Gates(v_, pro)
        tu = Turn(ga)
        dm = Delta("dmeta", tu, True)
        dd = Delta("delta", dm, False)
        zz = gate_z(dd)
        sc_ = short_conv(zz)
        bs = branch_sc(sc_)
        bd = branch_dn(bs)
        ou = residual("out", bd, me_hi, me_lo, [8], first=x_res)
        n2 = Norm("norm2", ou, x, "norm2", SEQ)
        gu = gate_up(n2)
        dn = residual("down", gu, y_hi, y_lo, [8, 8, 6])
        f1 = Norm("fin1", dn, x, "fin1", SEQ, plain=x)
        n3 = Norm("even", f1, x, "even", SEQ)
        gl = glu_conv(n3)
        bv = PoolDiff(gl)
        pm = pool_mix(bv)
        bg = gated("bgate", pm, yb, mx_hi, mx_lo, KT, lambda i: i + KT)
        ln = LayerNorm(bg)
        ag = gated("agate", ln, uc, mx_hi, mx_lo, KT)
        mi = residual("mix", ag, mx_hi, mx_lo, [8, 8])
        n4 = Norm("odd", mi, x, "odd", SEQ)
        xr = lru_conv(n4)
        lm = Lambda(xr)
        lr = lru(lm)
        lg = lru_scan(lr)
        lo = residual("lout", lg, xc_hi, xc_lo, [8, 4], final=True)
        f2 = Norm("fin2", lo, x, "fin2", SEQ, plain=x)
        Output(f2)

        block = ctx.enter_context(nc.Block())

        @block.sync
        def _(e):
            for s in stages:
                s.sp(e)

        @block.scalar
        def _(e):
            ticks[e] = e.alloc_register("act_tick")
            e.reg_mov(ticks[e], 0)
            for s in stages:
                s.act(e)

        @block.vector
        def _(e):
            for s in stages:
                s.dve(e)

        @block.gpsimd
        def _(e):
            ticks[e] = e.alloc_register("pool_tick")
            e.reg_mov(ticks[e], 0)
            for s in stages:
                s.pool(e)

        @block.tensor
        def _(e):
            for s in stages:
                s.pe(e)


def tiles_of(w):
    k, m = w.shape
    return w.reshape(k // P, P, m // P, P).transpose(2, 0, 1, 3)


def units_of(groups):
    u = np.zeros((len(groups), WT, P, P), np.float32)
    for n, g in enumerate(groups):
        u[n, :len(g)] = g
    return u.transpose(0, 2, 1, 3).reshape(len(groups), P, WT * P)


def weight_stream(i):
    f = {k: np.asarray(i[k]) for k in i}
    w_in = f["w_in"][0]
    c = np.cumsum([0, D, D, D, D, 16, 16, D, D, D, D, D])
    part = {n: tiles_of(w_in[:, c[j]:c[j + 1]]) for j, n in enumerate(["q", "k", "v", "z", "b", "a", "scb", "scc", "scx", "ga", "gb"]) if n not in "ba"}
    dn, sc, wo = (tiles_of(f[n][0]) for n in ("w_branch_dn", "w_branch_sc", "w_out"))
    gu, down = tiles_of(f["w_gate_up"][0]), tiles_of(f["w_down"][0])
    ev = tiles_of(f["w_in_even_2"][0])
    val, glu, ag, bv, bg = (ev[KT * j:KT * (j + 1)] for j in range(5))
    pw = [tiles_of(f["pool_w_2"][0, g]) for g in range(4)]
    mix, odd, lo = tiles_of(f["w_out_even_2"][0]), tiles_of(f["w_in_odd_2"][0]), tiles_of(f["w_out_odd_2"][0])
    rg, ig = f["w_rg_2"][0], f["w_ig_2"][0]
    s = {
        "q": list(part["q"]), "k": list(part["k"]), "v": list(part["v"]), "z": list(part["z"]),
        "sc": [part[n][t] for t in range(KT) for n in ("scc", "scx", "scb")],
        "bsc": [w[t] for t in range(KT) for w in (part["gb"], sc)],
        "bdn": [w[t] for t in range(KT) for w in (part["ga"], dn)],
        "out": list(wo), "gu": [gu[t + o] for t in range(FT) for o in (0, FT)],
        "down": [down[t, k:k + 8] for t in range(KT) for k in (0, 8, 16)],
        "glu": [w[t] for t in range(KT) for w in (val, glu)], "bval": list(bv),
        "pool": [[pw[g][m, k] for m in range(2) for k in range(2)] for g in range(4)],
        "bgate": list(bg), "agate": list(ag), "mix": [mix[t, k:k + 8] for t in range(KT) for k in (0, 8)],
        "xr": list(odd[:LT]), "lru": [[w[3 * g + q] for q in range(3) for w in (rg, ig)] for g in range(4)],
        "lgate": list(odd[LT:]), "lout": [lo[t, k:k + 8] for t in range(KT) for k in (0, 8)],
    }
    return units_of([u for name, n in UNITS for u in s[name]])


def params(i):
    src = {"norm1": "norm1_w", "sc": "sc_conv_w", "dnn": "dn_norm_w", "norm2": "norm2_w", "fin1": "final_norm_w",
           "even": "norm_even_2", "ca": "conv_a_w_2", "cab": "conv_a_b_2", "lng": "ln_a_g_2", "lnb": "ln_a_b_2",
           "pb": "pool_b_2", "psc": "pool_scale_2", "odd": "norm_odd_2", "cc": "conv_c_w_2", "ccb": "conv_c_b_2",
           "brg": "b_rg_2", "big": "b_ig_2", "lam": "lru_lambda_2", "fin2": "final_norm_2"}
    out = np.zeros((P, NPAR_PAD), np.float32)
    for name, n, k in PARAMS:
        if name in ("cq", "ck", "cv"):
            j = ("cq", "ck", "cv").index(name)
            v = np.asarray(i["dn_conv_w"])[0][:, j * D:(j + 1) * D]
        else:
            v = np.asarray(i[src[name]])
        o = PAR[name][0]
        out[:, o:o + n * k] = v.reshape(k, n, P).transpose(2, 1, 0).reshape(P, n * k)
    return out


def constants():
    r = np.arange(P)
    row, col = r[:, None], r[None, :]
    one = np.ones((P, P), np.float32)
    m = {"ident": row == col, "ones": one, "ones128": one * P, "mean1024": one / D, "mean128": one / P,
         "uf": row <= col, "vf": row > col, "ub": row >= col, "vb": row < col}
    for b in LEVELS:
        m[f"m{b}"] = (row // (2 * b) == col // (2 * b)) & (row // b != col // b)
    cf = np.stack([m[n].astype(np.float32) for n in CONSTS], 1)
    cb = np.stack([m["ident"], NEG * (row > col), NEG * (row < col)], 1).astype(mybir.dt.np(BF16))
    return cf, cb


def kernel(**inputs):
    import concourse.bacc as _bacc
    from concourse.bass_utils import run_bass_kernel_spmd as _run

    i = {k: np.asarray(v) for k, v in inputs.items()}
    cf, cb = constants()
    tok = np.concatenate([i["meta_tokens"], i["x"][0]], 0)
    small = np.ones((P, 128), np.float32)
    small[:, 124:127] = [EPS, P * EPS, 1e-5]
    small[:, 0:16] = i["A_log"].reshape(1, 16)
    small[:, 16:32] = i["dt_bias"].reshape(1, 16)
    for g, w in enumerate(POOLW):
        small[:, 48 + 16 * g:64 + 16 * g] = 1.0 / np.minimum(np.arange(1, 17), w)
    arrays = {
        "x": np.ascontiguousarray(tok.T.reshape(KT, P, T1).transpose(1, 0, 2)),
        "w": weight_stream(i),
        "wba": np.ascontiguousarray(i["w_in"][0][:, 4 * D:4 * D + 32].reshape(KT, P, 32).transpose(1, 0, 2)),
        "par": params(i), "cf": cf, "cb": cb, "small": small,
    }
    nc = _bacc.Bacc("TRN2", target_bir_lowering=False, num_devices=1)
    a = {n: nc.dram_tensor(f"in_{n}", v.shape, mybir.dt.from_np(v.dtype), kind="ExternalInput").ap() for n, v in arrays.items()}
    out = nc.dram_tensor("out_0", (P, KT, SEQ), F32, kind="ExternalOutput").ap()
    build(nc, a, out)
    r = _run(nc, [{f"in_{n}": v for n, v in arrays.items()}], core_ids=[0])
    got = r.results[0]["out_0"]
    return np.ascontiguousarray(got.transpose(2, 1, 0).reshape(1, SEQ, D))
```

```python
from contextlib import ExitStack

import numpy as np
import concourse.bass as bass
from concourse import mybir

F32 = mybir.dt.float32
F32R = mybir.dt.float32r
BF16 = mybir.dt.bfloat16
ALU = mybir.AluOpType
ACT = mybir.ActivationFunctionType

P = 128
D = 1024
KT = D // P
SEQ = 512
META = 16
T1 = META + SEQ
HALF = T1 // 2
H = 8
CH = 128
NCH = SEQ // CH
FF = 2816
FT = FF // P
LW = 1536
LT = LW // P
WT = 8
XP = 4
RAW = 4
EPS = 1e-6
NEG = -30000.0
LEVELS = [1, 2, 4, 8, 16, 32, 64]

UNITS = [("q", H), ("k", H), ("v", H), ("z", KT), ("sc", 3 * KT), ("bsc", 2 * KT), ("bdn", 2 * KT),
         ("out", KT), ("gu", 2 * FT), ("down", 3 * KT), ("glu", 2 * KT), ("bval", KT), ("pool", 4),
         ("agate", KT), ("bgate", KT), ("mix", 2 * KT), ("xr", LT), ("lru", 4), ("lgate", LT),
         ("lout", 2 * KT)]
BASE = {}
NU = 0
for _name, _n in UNITS:
    BASE[_name] = NU
    NU += _n
    assert _n % RAW == 0

PARAMS = [("norm1", KT, 1), ("cq", H, 5), ("ck", H, 5), ("cv", H, 5), ("sc", KT, 3), ("dnn", 1, 1),
          ("norm2", KT, 1), ("fin1", KT, 1), ("even", KT, 1), ("ca", KT, 31), ("cab", KT, 1),
          ("lng", KT, 1), ("lnb", KT, 1), ("pb", KT, 1), ("psc", KT, 1), ("odd", KT, 1), ("cc", LT, 4),
          ("ccb", LT, 1), ("brg", LT, 1), ("big", LT, 1), ("lam", LT, 1), ("fin2", KT, 1)]
PAR = {}
NPAR = 0
for _name, _n, _k in PARAMS:
    PAR[_name] = (NPAR, _n, _k)
    NPAR += _n * _k
NPAR_PAD = NPAR + (-NPAR) % 8

CONSTS = ["ident", "ones", "ones128", "mean1024", "mean128", "uf", "vf", "ub", "vb"] + [f"m{b}" for b in LEVELS]
CIDX = {n: i for i, n in enumerate(CONSTS)}
POOLW = [2, 4, 8, 16]


class Steps:

    def __init__(self, sem, names):
        self.sem, self.names, self.n = sem, list(names), len(names)
        self.at = {k: i for i, k in enumerate(self.names)}
        self.next = 0
        assert len(self.at) == self.n

    def open(self, e):
        e.sem_inc(self.sem, self.n)

    def done(self, ins, step):
        assert self.names[self.next % self.n] == step, (step, self.names[self.next % self.n])
        self.next += 1
        ins.then_inc(self.sem, 1)

    def count(self, it, step, back=0):
        return it * self.n + (1 - back) * self.n + self.at[step] + 1


def build(nc, a, out):
    ctx = ExitStack()
    with ctx:
        def sem(name):
            return ctx.enter_context(nc.semaphore(name))

        start = nc.sbuf_base + (-nc.sbuf_base) % 32
        top = [start]

        def at(name, shape, offset, dt=F32):
            return nc.alloc_sbuf_tensor_at(name, shape, dt, offset=offset)

        def put(name, shape, dt=F32):
            n = int(np.prod(shape[1:])) * (2 if dt == BF16 else 4)
            t = at(name, shape, top[0], dt)
            top[0] += n + (-n) % 32
            return t

        w_raw = put("w_raw", [P, RAW, WT * P])
        w_hi = put("w_hi", [P, 2, WT * P], F32R)
        w_lo = put("w_lo", [P, 2, WT * P], F32R)
        h_hi = put("h_hi", [P, KT, T1], F32R)
        h_lo = put("h_lo", [P, KT, T1], F32R)
        par = put("par", [P, NPAR_PAD])
        cf = put("cf", [P, len(CONSTS), P])
        cb = put("cb", [P, 3, P], BF16)
        small = put("small", [P, 128])
        z0 = top[0]
        K16 = 16384

        def z(name, shape, off, dt=F32):
            n = int(np.prod(shape[1:])) * 4
            assert z0 + off + n <= nc.sbuf_usable_end, (name, z0 + off + n, nc.sbuf_usable_end)
            return at(name, shape, z0 + off, dt)

        oT = z("oT", [P, H, SEQ], 0)
        qT = z("qT", [P, H, T1], K16)
        kT = z("kT", [P, H, T1], K16 + 16896)
        dl = K16 + 2 * 16896
        x_in = z("x_in", [P, KT, T1], dl)
        v_tok = z("v_tok", [P, NCH, H, P], dl)
        k_tok = z("k_tok", [P, NCH, H, P], dl + K16)
        v_met = z("v_met", [P, H, P], dl + 2 * K16)
        k_met = z("k_met", [P, H, P], dl + 2 * K16 + 4096)
        st = z("st", [P, 2, H, P], dl + 2 * K16 + 8192)
        tb = dl + 2 * K16 + 16384
        NB = NCH + 1
        beta = z("beta", [P, NB, 2 * H], tb)
        gdec = z("gdec", [P, NB, 2 * H], tb + 320)
        ecol = z("ecol", [P, NB, 2 * H], tb + 640)
        kcol = z("kcol", [P, NB, 2 * H], tb + 960)
        lcol = z("lcol", [P, NB, 2 * H], tb + 1280)
        tmpc = z("tmpc", [P, 4, NB * 2 * H], 13312)
        wk = tb + 1600
        vT = z("vT", [P, H, T1], wk)
        HG = 4
        work = {}
        for _i, _n in enumerate(["dec", "a", "e", "x", "xt", "tt", "kc", "eg"]):
            work[_n] = z(f"wk_{_n}", [P, 2, HG, P], wk + _i * 4096)
        work["kd"] = z("wk_kd", [P, 2, HG, P], dl + 2 * K16)
        work["r"] = z("wk_r", [P, 2, HG, P], dl + 2 * K16 + 4096)
        b_now = small[:, 32:40].rearrange("p (s u) -> p s u", s=2)
        g_now = small[:, 112:120].rearrange("p (s u) -> p s u", s=2)
        cin = z("cin", [P, 2, T1 + 4], 0)
        cacc = z("cacc", [P, 2, T1], 4256)
        sqv = z("sqv", [P, 2, T1], 8704)
        rrow = z("rrow", [P, T1], dl + 2 * K16 + 8192)
        rbuf = z("rbuf", [P, 4, T1], dl + 2 * K16 + 8192)
        ba_f = z("ba_f", [32, T1], dl + 2 * K16 + 8192 + 2 * T1 * 4)
        hf0 = z("hf0", [P, 2, T1], wk)
        wba = z("wba", [P, KT, P], wk + 20000)
        wba_hi = z("wba_hi", [P, KT, P], wk + 20000 + 4096, F32R)
        wba_lo = z("wba_lo", [P, KT, P], wk + 20000 + 8192, F32R)

        zs = z("zs", [P, KT, SEQ], K16)
        od_hi = z("od_hi", [P, KT, SEQ], 2 * K16, F32R)
        od_lo = z("od_lo", [P, KT, SEQ], 3 * K16, F32R)
        sc_hi = z("sc_hi", [P, KT, SEQ], 4 * K16, F32R)
        sc_lo = z("sc_lo", [P, KT, SEQ], 5 * K16, F32R)
        m1 = z("m1", [P, KT, SEQ], 6 * K16)
        me_hi = z("me_hi", [P, KT, SEQ], 0, F32R)
        me_lo = z("me_lo", [P, KT, SEQ], K16, F32R)
        tz = 7 * K16
        tmp = z("tmp", [P, 8, SEQ + 32], tz)
        x_res = z("x_res", [P, KT, SEQ], 4 * K16)
        x = z("x", [P, KT, SEQ], 6 * K16)
        y_hi = z("y_hi", [P, FT, SEQ], 0, F32R)
        y_lo = z("y_lo", [P, FT, SEQ], FT * SEQ * 4, F32R)
        uc = z("uc", [P, KT, SEQ], 0)
        mx_hi = z("mx_hi", [P, 2 * KT, SEQ], K16, F32R)
        mx_lo = z("mx_lo", [P, 2 * KT, SEQ], 3 * K16, F32R)
        u_in = z("u_in", [P, KT, SEQ], K16)
        sg_a = z("sg_a", [P, KT, SEQ], 3 * K16)
        yb = z("yb", [P, KT, SEQ], 5 * K16)
        xc = z("xc", [P, LT, SEQ], 0)
        L24 = LT * SEQ * 4
        xc_hi = z("xc_hi", [P, LT, SEQ], L24, F32R)
        xc_lo = z("xc_lo", [P, LT, SEQ], 2 * L24, F32R)
        hs = z("hs", [P, LT, SEQ], 3 * L24)

        ps = ctx.enter_context(nc.psum_tensor("ps", [P, 8, 512], F32))

        def cmat(name):
            return cf[:, CIDX[name], :]

        def pcol(name, tile, tap=0):
            o, n, k = PAR[name]
            return par[:, o:o + n * k].rearrange("p (n k) -> p n k", k=k)[:, tile, tap:tap + 1]

        eps_col = small[:, 124:125]
        s_raw = [sem(f"s_raw{j}") for j in range(RAW)]
        s_x = [sem(f"s_x{q}") for q in range(XP)]
        s_hi, s_lo, s_pe = sem("s_hi"), sem("s_lo"), sem("s_pe")
        s_cst, s_xr, s_out = sem("s_cst"), sem("s_xr"), sem("s_out")
        s_zero = sem("s_zero")
        ticks = {}

        def wait(e, st_, it, step, back=0):
            n = st_.count(it, step, back)
            e.wait_ge(st_.sem, n)
            settle(e, n)

        def settle(e, n):
            if not isinstance(n, int) and e in ticks:
                e.reg_add(ticks[e], ticks[e], 1)

        def loop(e, n, body, iter0=0):
            if n == 1:
                body(iter0)
            else:
                with e.Fori(iter0, iter0 + n) as it:
                    body(it)

        def round_unit(e, u, c):
            j = c % RAW
            div = (u - j) if isinstance(u, int) else None
            n = 16 * (div // RAW + 1) if div is not None else (u - j) * (16 // RAW) + 16
            e.wait_ge(s_raw[j], n)
            if not (isinstance(u, int) and u < 2):
                e.wait_ge(s_pe, u - 1)
            settle(e, n)
            e.activation(w_hi[:, j % 2, :], w_raw[:, j, :], ACT.Copy).then_inc(s_hi, 1)

        def split_unit(e, u, c):
            e.wait_ge(s_hi, u + 1)
            settle(e, u)
            e.tensor_tensor(w_lo[:, c % 2, :], w_raw[:, c % RAW, :], w_hi[:, c % 2, :].bitcast(F32),
                            ALU.subtract).then_inc(s_lo, 1)

        K8 = [(t, t) for t in range(KT)]
        stages = []

        class Stage:

            def __init__(self, name, before):
                self.name, self.before, self.log = name, before, {}
                stages.append(self)

            def steps(self, eng, names, iters=1):
                s = Steps(sem(f"s_{self.name}_{eng}"), names)
                s.iters = iters
                self.log[eng] = s
                return s

            def wait_whole(self, e, engs=("act", "dve", "pool", "pe")):
                for g in engs:
                    for key, st_ in self.log.items():
                        if g in (key, key[0]):
                            e.wait_ge(st_.sem, (st_.iters + 1) * st_.n)

            def open(self, e, eng):
                for key, st_ in self.log.items():
                    if eng in (key, key[0]):
                        st_.open(e)

            def begin(self, e, eng):
                if self.before is not None:
                    self.before.wait_whole(e)

            def on(self, e, eng, it, step, back=0):
                wait(e, self.log[eng], it, step, back)

            def did(self, eng, ins, step):
                self.log[eng].done(ins, step)

            def psum_read(self, e):
                self.wait_whole(e, ("act", "dve", "pool"))

            def sp(self, e): pass
            def pe(self, e): pass
            def act(self, e): pass
            def dve(self, e): pass
            def pool(self, e): pass

        class Linear(Stage):

            def __init__(self, name, before, n, m, units, banks, freed, prog, width=((META, T1),), final=False,
                         after=None, feed=None, start=None):
                super().__init__(name, before)
                self.after, self.feed = after, feed or []
                self.n, self.m, self.units, self.banks, self.freed = n, m, units, banks, freed
                self.prog, self.width, self.final, self.start = prog, width, final, start or {}
                self.per = m * len(units)
                self.order = {}
                for eng in ("act", "dve", "pool", "pe"):
                    mine = [q for q in prog if q[0] == eng]

                    def of(q, j):
                        lag = q[4] if len(q) == 5 else 0
                        if isinstance(lag, dict):
                            return lag.get(j, [])
                        if lag == "end":
                            return [m - 1] if j == m + 2 else []
                        return [j - lag] if 0 <= j - lag < m else []
                    order = []
                    for j in range(m + 3):
                        order += [(q, k) for q in mine for k in of(q, j)]
                        if j < m:
                            order.append((None, j))
                    self.order[eng] = order
                    if mine:
                        self.steps(eng, [(q[1], j) for q, j in order if q], n)

            def last_unit(self, output):
                return max(i for i, q in enumerate(self.units) if q[0] == output)

            def needs(self, q):
                u = 0
                for w in q[2]:
                    if w[0] == "out":
                        u = max(u, self.last_unit(w[1]))
                    elif w[2] == 0:
                        u = max([u] + [self.needs(p_) for p_ in self.prog if p_[:2] == w[:2] and len(p_) == 4])
                return u

            def back(self, j, k):
                assert k <= self.m
                return ((j - k) % self.m, int(j < k))

            def await_(self, e, it, j, what):
                if what[0] == "out":
                    u = self.last_unit(what[1])
                    n = it * self.per + (BASE[self.name] + j * len(self.units) + u + 1)
                    e.wait_ge(s_pe, n)
                    settle(e, n)
                else:
                    eng, step, k = what
                    if isinstance(k, str) and k[0] == "#":
                        self.on(e, eng, it, (step, int(k[1:])))
                        return
                    jj, b = (self.m - 1, 1) if k == "end" else self.back(j, k)
                    self.on(e, eng, it, (step, jj), b)

            def emit(self, e, eng, it, q, j):
                for w in q[2]:
                    self.await_(e, it, j, w)
                self.it = it
                self.did(eng, q[3](e, it * self.m + j, j), (q[1], j))

            def side(self, e, eng, prepare):
                self.begin(e, eng)
                if eng in self.start:
                    self.start[eng](e)
                nu = len(self.units)
                before_gemm = [q for q in self.prog if q[0] == eng and q[1].startswith("pre")]

                def body(it):
                    ready = [0]

                    def ahead(last):
                        while ready[0] <= last and prepare is not None:
                            c = ready[0] + 2
                            ready[0] += 1
                            w = it * self.per + (BASE[self.name] + c)
                            if not (isinstance(w, int) and w >= NU):
                                prepare(e, w, c)
                    slot, seen = 0, 0
                    for q, j in self.order[eng]:
                        if q is None:
                            ahead(j * nu + nu - 1)
                            slot, seen = j + 1, 0
                        elif q not in before_gemm and slot < self.m:
                            if j == slot and len(q) == 4:
                                seen = max(seen, self.needs(q))
                            ahead(slot * nu + seen)
                        if q is not None:
                            self.emit(e, eng, it, q, j)
                self.run(e, body)

            def run(self, e, body):
                loop(e, self.n - int(self.final), body)
                if self.final:
                    body(self.n - 1)

            def psum_read(self, e):
                for eng, step, _ in self.freed.values():
                    self.on(e, eng, self.n - 1, (step, self.m - 1))

            def act(self, e):
                self.side(e, "act", round_unit)

            def dve(self, e):
                self.side(e, "dve", None)

            def pool(self, e):
                self.side(e, "pool", split_unit)

            def pe(self, e):
                if self.after is None:
                    self.before.wait_whole(e, ("act", "dve", "pool"))
                else:
                    self.after.psum_read(e)
                nu = len(self.units)

                def body(it):
                    for j in range(self.m):
                        for u, (o, hi, lo, tiles, first, last) in enumerate(self.units):
                            if first:
                                self.await_(e, it, j, self.freed[o])
                            outs = self.banks(j, o)
                            width = self.width[o] if isinstance(self.width, dict) else self.width
                            if len(tiles) and isinstance(tiles[0], list):
                                groups = tiles
                            else:
                                groups = [tiles]
                            e.wait_ge(s_lo, it * self.per + (BASE[self.name] + j * nu + u + 1))
                            s = (j * nu + u) % 2
                            for g, tl in enumerate(groups):
                                gouts = outs if len(groups) == 1 else outs[g]
                                for n, (t, k) in enumerate(tl):
                                    for t_, maker in self.feed:
                                        if t_ is hi and (callable(k) or j == 0):
                                            made = maker(k(j) if callable(k) else k)
                                            if made is not None:
                                                made[0].on(e, "pool", made[1], made[2])
                                    wh, wl = w_hi[:, s, t * P:(t + 1) * P], w_lo[:, s, t * P:(t + 1) * P]
                                    for p3, (w, r) in enumerate(((wh, hi), (wh, lo), (wl, hi))):
                                        for v, ov in enumerate(gouts):
                                            t0, t1 = width[v]
                                            kk = k(j) if callable(k) else k
                                            mm = e.matmul(ov, w, r[:, kk, t0:t1], start=(first and n == 0 and p3 == 0),
                                                          stop=(last and n == len(tl) - 1 and p3 == 2))
                            mm.then_inc(s_pe, 1)
                        cut = self.order["pe"].index((None, j))
                        past = self.order["pe"].index((None, j - 1)) if j else -1
                        for q, jj in self.order["pe"][past + 1:cut]:
                            self.emit(e, "pe", it, q, jj)
                    for q, jj in self.order["pe"][cut + 1:]:
                        self.emit(e, "pe", it, q, jj)
                self.run(e, body)

        class Prologue(Stage):
            def __init__(self):
                super().__init__("pro", None)
                self.steps("dve", ["halo0", "halo1", "wlo"])
                self.steps("act", ["whi"])

            def act(self, e):
                e.dma_start(small[:], a["small"]).then_inc(s_cst, 16)
                e.dma_start(par[:], a["par"]).then_inc(s_cst, 16)

            def dve(self, e):
                self.did("dve", e.memset(cin[:, :, 0:2], 0.0), "halo0")
                self.did("dve", e.memset(cin[:, :, T1 + 2:T1 + 4], 0.0), "halo1")

            def first_act(self, e):
                for u in range(2):
                    round_unit(e, u, u)
                e.wait_ge(s_cst, 80)
                self.did("act", e.activation(wba_hi[:], wba[:], ACT.Copy), "whi")

            def first_pool(self, e):
                for u in range(2):
                    split_unit(e, u, u)

            def first_dve(self, e):
                self.on(e, "act", 0, "whi")
                self.did("dve", e.tensor_tensor(wba_lo[:], wba[:], wba_hi[:].bitcast(F32), ALU.subtract), "wlo")

            def sp(self, e):
                for q in range(XP):
                    k = slice(q * KT // XP, (q + 1) * KT // XP)
                    e.dma_start(x_in[:, k, :], a["x"][:, k, :]).then_inc(s_x[q], 16)
                e.dma_start(cf[:], a["cf"]).then_inc(s_cst, 16)
                for u in range(RAW):
                    if u == 2:
                        e.dma_start(cb[:], a["cb"]).then_inc(s_cst, 16)
                        e.dma_start(wba[:], a["wba"]).then_inc(s_cst, 16)
                    e.dma_start(w_raw[:, u, :], a["w"][u]).then_inc(s_raw[u], 16)

                def body(it):
                    for j in range(RAW):
                        e.wait_ge(s_lo, it * RAW + (j + 1 - RAW))
                        e.dma_start(w_raw[:, j, :], a["w"][it * RAW + j]).then_inc(s_raw[j], 16)
                loop(e, NU // RAW - 1, body, 1)

        def row(i, n=SEQ, off=0):
            return tmp[:, i, off:off + n]

        class Norm(Stage):

            def __init__(self, name, before, src, w, tokens, plain=None, hf=None, sq=None, rr=None, acc=None, w0=None, pro=None):
                super().__init__(name, before)
                self.pro = pro
                self.src, self.w, self.t, self.plain, self.w0 = src, w, tokens, plain, w0
                self.sums = isinstance(before, Linear)
                self.views = [(0, HALF), (HALF, T1)] if tokens == T1 else [(0, tokens)]
                self.hf = hf if hf is not None else tmp[:, 0:2, 0:SEQ]
                self.sq = sq if sq is not None else tmp[:, 2:4, 0:SEQ]
                self.rr = rr if rr is not None else row(3)
                self.acc = acc if acc is not None else row(4)
                self.o = 0 if tokens == T1 else META
                split = plain is None
                K = range(KT)
                self.steps("act", [("sq", k) for k in K if not self.sums] + ["rt0"] * bool(w0) + ["rt"] + [("hi", k) for k in K if split])
                self.steps("pe", ["ss0"] * bool(w0) + ["ss"])
                if w0:
                    self.steps("dve", ["r0", "r0sq", "ms", ("x0", 0), ("x0", 1), "r"] + [q for k in K for q in [("h", k)] + [("x0", k + 2)] * (k + 2 < KT)])
                else:
                    self.steps("dve", [("add", k) for k in K if k and not self.sums] + ["r"] + [("h", k) for k in K])
                if split:
                    self.steps("pool", [("lo", k) for k in K])

            def loaded(self, e, k=None):
                if self.src is x_in:
                    for q in range(XP) if k is None else [k * XP // KT]:
                        e.wait_ge(s_x[q], 16)
                    if k is None:
                        e.wait_ge(s_cst, 80)

            def psum_read(self, e):
                self.on(e, "act", 0, "rt")

            def act(self, e):
                self.begin(e, "act")
                if not self.sums:
                    for k in range(KT):
                        self.loaded(e, k)
                        if k > 2:
                            self.on(e, "dve", 0, ("add", k - 2))
                        dst = self.acc if k == 0 else self.sq[:, k % 2, 0:self.t]
                        self.did("act", e.activation(dst, self.src[:, k, 0:self.t], ACT.Square), ("sq", k))
                if self.pro is not None:
                    self.pro.first_act(e)
                self.on(e, "pe", 0, "ss")
                if self.w0:
                    self.did("act", e.activation(row(5), ps[:, 5, :], ACT.Sqrt, bias=eps_col), "rt0")
                    self.on(e, "dve", 0, "ms")
                    self.did("act", e.activation(self.rr, row(7), ACT.Sqrt, bias=eps_col), "rt")
                else:
                    nb, w = len(self.views), self.views[0][1]
                    self.did("act", e.activation(self.rr[:, 0:self.t].rearrange("p (b n) -> p b n", b=nb), ps[:, 4:4 + nb, 0:w],
                                                 ACT.Sqrt, bias=eps_col), "rt")
                if self.plain is None:
                    for k in range(KT):
                        self.on(e, "dve", 0, ("h", k))
                        self.did("act", e.activation(h_hi[:, k, self.o:self.o + self.t], self.hf[:, k % 2, 0:self.t], ACT.Copy), ("hi", k))

            def pe(self, e):
                self.begin(e, "pe")
                self.loaded(e)
                if not self.sums:
                    self.on(e, "dve", 0, ("add", KT - 1))
                if self.w0:
                    mean = cmat("mean1024")
                    self.did("pe", e.matmul(ps[:, 4, :], mean, row(7), start=True, stop=True), "ss0")
                    self.did("pe", e.matmul(ps[:, 5, :], mean, row(4), start=True, stop=True), "ss")
                else:
                    for b, (lo, hi) in enumerate(self.views):
                        mm = e.matmul(ps[:, 4 + b, 0:hi - lo], cmat("mean1024"), self.acc[:, lo:hi], start=True, stop=True)
                    self.did("pe", mm, "ss")

            def dve(self, e):
                self.begin(e, "dve")
                if not self.sums:
                    for k in range(1, KT):
                        self.on(e, "act", 0, ("sq", k))
                        if k > 1:
                            self.on(e, "dve", 0, ("add", k - 1))
                        self.did("dve", e.tensor_tensor(self.acc, self.acc, self.sq[:, k % 2, 0:self.t], ALU.add), ("add", k))
                    self.loaded(e)

                def x0(k):
                    self.did("dve", e.scalar_tensor_tensor(x[:, k, :], x[:, k, :], pcol(self.w0, k), row(5), ALU.mult, ALU.mult), ("x0", k))
                if self.w0:
                    self.on(e, "act", 0, "rt0")
                    self.did("dve", e.reciprocal(row(5), row(5)), "r0")
                    self.on(e, "dve", 0, "r0")
                    self.did("dve", e.tensor_tensor(row(6), row(5), row(5), ALU.mult), "r0sq")
                    self.on(e, "dve", 0, "r0sq")
                    self.did("dve", e.tensor_tensor(row(7), row(6), ps[:, 4, :], ALU.mult), "ms")
                    x0(0)
                    x0(1)
                self.on(e, "act", 0, "rt")
                self.did("dve", e.reciprocal(self.rr[:, 0:self.t], self.rr[:, 0:self.t]), "r")
                self.on(e, "dve", 0, "r")
                for k in range(KT):
                    if self.plain is None and k > 1:
                        self.on(e, "pool", 0, ("lo", k - 2))
                    if self.w0:
                        self.on(e, "dve", 0, ("x0", k))
                    dst = self.hf[:, k % 2, 0:self.t] if self.plain is None else self.plain[:, k, :]
                    self.did("dve", e.scalar_tensor_tensor(dst, self.src[:, k, 0:self.t], pcol(self.w, k), self.rr[:, 0:self.t], ALU.mult, ALU.mult), ("h", k))
                    if self.w0 and k + 2 < KT:
                        x0(k + 2)
                if self.pro is not None:
                    self.pro.first_dve(e)

            def pool(self, e):
                if self.plain is None:
                    self.begin(e, "pool")
                    if self.pro is not None:
                        self.pro.first_pool(e)
                    for k in range(KT):
                        self.on(e, "act", 0, ("hi", k))
                        o = self.o
                        self.did("pool", e.tensor_tensor(h_lo[:, k, o:o + self.t], self.hf[:, k % 2, 0:self.t], h_hi[:, k, o:o + self.t].bitcast(F32), ALU.subtract), ("lo", k))

        def from_norm(n_):
            return lambda k: (n_, 0, ("lo", k))

        def from_items(l, off=0):
            return lambda k: (l, (k - off) // l.m, ("lo", (k - off) % l.m)) if k >= off else None

        two = ((0, HALF), (HALF, T1))

        def pair(v):
            return v.rearrange("p (b n) -> p b n", b=2)

        def qkv(name, before, cw, dst, side, side_ones):
            prog = []
            silu = "silu" if side is None else "presilu"
            if side is not None:
                bias = small[:, 125:126] if side_ones == "ones128" else eps_col
                prog += [
                    ("act", "prert", [("pe", "ss", 0), ("pool", "prenrm", 2)], lambda e, i, j: e.activation(
                        pair(rbuf[:, j % 2, :]), ps[:, 4:6, 0:HALF], ACT.Sqrt, bias=bias), 1),
                    ("act", "presq", [("pe", "ss", 2)], lambda e, i, j: e.activation(sqv[:, j % 2, :], side[:, i, :], ACT.Square)),
                    ("pe", "ss", [("act", "presq", 0), ("act", "prert", 1)], lambda e, i, j: [
                        e.matmul(ps[:, 4 + v, 0:HALF], cmat(side_ones), sqv[:, j % 2, v * HALF:(v + 1) * HALF], start=True, stop=True)
                        for v in range(2)][-1]),
                    ("dve", "rec", [("act", "prert", 0)], lambda e, i, j: e.reciprocal(rbuf[:, j % 2, :], rbuf[:, j % 2, :]), 1),
                    ("pool", "prenrm", [("dve", "rec", 0)], lambda e, i, j: e.tensor_tensor(
                        side[:, i, :], side[:, i, :], rbuf[:, j % 2, :], ALU.mult), 1),
                ]
            prog.append(("act", silu, [("dve", "c4", 0)], lambda e, i, j: e.activation(dst[:, i, :], cacc[:, j % 2, :], ACT.Silu), 1))
            prog.append(("act", "evac", [("dve", "c4", 2), ("out", 0)], lambda e, i, j: e.activation(
                pair(cin[:, j % 2, 2:2 + T1]), ps[:, 2 * (j % 2):2 * (j % 2) + 2, 0:HALF], ACT.Copy)))

            def tap(t):
                if t == 0:
                    return ("dve", "c0", [("act", "evac", 0), ("act", silu, 2)], lambda e, i, j: e.tensor_scalar(
                        cacc[:, j % 2, :], cin[:, j % 2, 0:T1], pcol(cw, i), None, ALU.mult))
                return ("dve", f"c{t}", [("dve", f"c{t - 1}", 0)], lambda e, i, j: e.scalar_tensor_tensor(
                    cacc[:, j % 2, :], cin[:, j % 2, t:t + T1], pcol(cw, i, t), cacc[:, j % 2, :], ALU.mult, ALU.add))
            prog += [tap(t) for t in range(5)]
            return Linear(name, before, H // 8, 8, [(0, h_hi, h_lo, K8, True, True)],
                          lambda j, o: [ps[:, 2 * (j % 2) + v, 0:HALF] for v in range(2)],
                          {0: ("act", "evac", 2)}, prog, width=two, after=before,
                          feed=[(h_hi, from_norm(before))] if side is None else None,
                          start={"dve": lambda e: pro.wait_whole(e, ("dve",))} if side is None else None)

        SERIES = 9

        def log1p_steps(tag):
            return [(tag, n) for n in ["den", "rec", "z", "z2", "a0"] + list(range(1, SERIES - 1)) + ["end"]]

        def log1p(e, st_, tag, y, t1, t2):
            names = log1p_steps(tag)
            c = [2.0 / (2 * k + 1) for k in range(SERIES)]
            todo = [lambda: e.tensor_scalar(t1, y, 2.0, None, ALU.add),
                    lambda: e.reciprocal(t2, t1),
                    lambda: e.tensor_tensor(y, y, t2, ALU.mult),
                    lambda: e.tensor_tensor(t1, y, y, ALU.mult),
                    lambda: e.tensor_scalar(t2, t1, c[SERIES - 1], None, ALU.mult)]
            for k in range(SERIES - 2, 0, -1):
                todo.append(lambda k=k: e.scalar_tensor_tensor(t2, t2, c[k], t1, ALU.add, ALU.mult))
            todo.append(lambda: e.scalar_tensor_tensor(y, t2, c[0], y, ALU.add, ALU.mult))
            for f, name in zip(todo, names):
                st_.did("dve", f(), name)
                st_.on(e, "dve", 0, name)

        class Gates(Stage):

            def __init__(self, before, pro):
                super().__init__("gates", before)
                self.pro = pro
                self.steps("pe", ["ba", "bat"])
                self.steps("dve", ["b", "a", "neg", "abs"] + log1p_steps("l") + ["sp", "g"])
                self.steps("act", ["bac", "sig", "eA", "ex"])

            def pe(self, e):
                self.pro.wait_whole(e, ("dve",))
                for k in range(KT):
                    for p3, (l, r) in enumerate(((wba_hi, h_hi), (wba_hi, h_lo), (wba_lo, h_hi))):
                        for v in range(2):
                            m = e.matmul(ps[:, 6 + v, 0:HALF], l[:, k, :], r[:, k, v * HALF:(v + 1) * HALF],
                                         start=(k == 0 and p3 == 0), stop=(k == KT - 1 and p3 == 2))
                self.did("pe", m, "ba")
                self.before.wait_whole(e, ("act",))
                self.on(e, "act", 0, "bac")
                for c in range(NB):
                    t0 = META + (c - 1) * CH if c else 0
                    m = e.transpose(ps[:, 4, 32 * c:32 * c + 32], ba_f[:, t0:t0 + P], cmat("ident")[0:32, 0:32])
                self.did("pe", m, "bat")

            def dve(self, e):
                self.begin(e, "dve")
                ba = ps[:, 4, 0:32 * NB].rearrange("p (c n) -> p c n", c=NB)
                t = [tmpc[:, i, :] for i in range(4)]
                t0 = t[0].rearrange("p (c n) -> p c n", c=NB)
                dt = small[:, 16:32].unsqueeze(1).to_broadcast([P, NB, 16])
                ea = small[:, 32:48].unsqueeze(1).to_broadcast([P, NB, 16])
                self.on(e, "pe", 0, "bat")
                self.did("dve", e.tensor_copy(beta[:], ba[:, :, 0:16]), "b")
                self.did("dve", e.tensor_tensor(t0, ba[:, :, 16:32], dt, ALU.add), "a")
                self.on(e, "dve", 0, "a")
                self.did("dve", e.tensor_scalar(t[1], t[0], -1.0, None, ALU.mult), "neg")
                self.on(e, "dve", 0, "neg")
                self.did("dve", e.tensor_tensor(t[1], t[1], t[0], ALU.min), "abs")
                self.on(e, "act", 0, "ex")
                log1p(e, self, "l", t[1], t[2], t[3])
                self.did("dve", e.scalar_tensor_tensor(t[0], t[0], 0.0, t[1], ALU.max, ALU.add), "sp")
                self.on(e, "dve", 0, "sp")
                self.on(e, "act", 0, "eA")
                self.did("dve", e.scalar_tensor_tensor(gdec[:], t0, -1.0, ea, ALU.mult, ALU.mult), "g")

            def act(self, e):
                self.begin(e, "act")
                self.on(e, "pe", 0, "ba")
                self.did("act", e.activation(pair(ba_f[:]), ps[0:32, 6:8, 0:HALF], ACT.Copy), "bac")
                self.on(e, "dve", 0, "b")
                self.did("act", e.activation(beta[:], beta[:], ACT.Sigmoid), "sig")
                self.did("act", e.activation(small[:, 32:48], small[:, 0:16], ACT.Exp), "eA")
                self.on(e, "dve", 0, "abs")
                self.did("act", e.activation(tmpc[:, 1, :], tmpc[:, 1, :], ACT.Exp), "ex")

        class Decays(Stage):

            def __init__(self, before, ga):
                super().__init__("decays", before)
                self.ga = ga
                self.places = (("ecol", ("uf", "ub"), 5, 0, ecol), ("kcol", ("vf", "vb"), 5, 128, kcol), ("lcol", ("ones", "ones"), 4, 256, lcol))
                self.steps("pe", [q[0] for q in self.places])
                self.steps("act", [q[0] for q in self.places])

            def pe(self, e):
                self.ga.wait_whole(e, ("dve", "act"))
                for step, mats, bank, o, _ in self.places:
                    for c in range(NB):
                        n = P if c else META
                        for d in range(2):
                            col = o + c * 2 * H + d * H
                            m = e.matmul(ps[:, bank, col:col + H], cmat(mats[d])[0:n, :], gdec[0:n, c, d * H:(d + 1) * H], start=True, stop=True)
                    self.did("pe", m, step)

            def act(self, e):
                self.begin(e, "act")
                self.on(e, "pe", 0, "lcol")
                for step, _, bank, o, dst in self.places:
                    self.did("act", e.activation(dst[:], ps[:, bank, o:o + 2 * H * NB].rearrange("p (c n) -> p c n", c=NB), ACT.Exp), step)

        class Turn(Stage):

            def __init__(self, before, vs, ga):
                super().__init__("turn", before)
                self.vs, self.ga = vs, ga
                self.pairs = (0, 2, 6)

                self.hb = [(t, h) for h in range(H) for t in "kv"]
                self.steps("pe", [("t", i) for i in range(2 * H)])
                self.steps("act", [("m", i) for i in range(2 * H)])
                self.steps("dve", [("c", i) for i in range(2 * H)])
                self.steps("pool", ["o0", "s0"])

            def pe(self, e):
                self.vs.wait_whole(e)
                for i, (t, h) in enumerate(self.hb):
                    src = kT if t == "k" else vT
                    b = self.pairs[i % 3]
                    if i == 2:
                        self.ga.on(e, "act", 0, "bac")
                    if i > 2:
                        self.on(e, "act", 0, ("m", i - 3))
                        self.on(e, "dve", 0, ("c", i - 3))
                    for c in range(NCH):
                        e.transpose(ps[:, b, c * P:(c + 1) * P], src[:, h, META + c * CH:META + (c + 1) * CH], cmat("ident"))
                    m = e.transpose(ps[0:META, b + 1, 0:P], src[:, h, 0:META], cmat("ident"))
                    self.did("pe", m, ("t", i))

            def dve(self, e):
                self.begin(e, "dve")
                for i, (t, h) in enumerate(self.hb):
                    self.on(e, "pe", 0, ("t", i))
                    dst = k_tok if t == "k" else v_tok
                    self.did("dve", e.tensor_copy(dst[:, :, h, :], ps[:, self.pairs[i % 3], :].rearrange("p (c n) -> p c n", c=NCH)), ("c", i))

            def act(self, e):
                self.begin(e, "act")
                for i, (t, h) in enumerate(self.hb):
                    self.on(e, "pe", 0, ("t", i))
                    dst = k_met if t == "k" else v_met
                    self.did("act", e.activation(dst[0:META, h, :], ps[0:META, self.pairs[i % 3] + 1, 0:P], ACT.Copy), ("m", i))

            def pool(self, e):
                self.begin(e, "pool")
                self.did("pool", e.memset(oT[:], 0.0), "o0")
                self.did("pool", e.memset(st[:, 1], 0.0), "s0")

        class Delta(Stage):

            PERIOD, SHIFT = 73.1, 13.52
            TIMES = {"act": {"gc": 4.1, "bc": 5, "kc": 9.5, "eg": 10.2, "dec": 11.2, "xt1": 35.6, "tt2": 37.5,
                        "tt4": 41.9, "tt8": 49.6, "tt16": 52.5, "tt32": 64, "tt64": 68.7},
                     "dve": {"a": 0, "e1": 1.7, "x1": 4.2, "qk": 13.1, "xt2": 21.3, "x2": 25, "xt4": 29.5, "r": 29.6,
                        "x4": 30.9, "xt8": 33.8, "x8": 34.2, "xt16": 40.7, "x16": 43.6, "xt32": 47.5,
                        "x32": 51.3, "x64": 56.8, "vn": 59.1, "o": 63.8, "s": 67.6},
                     "pool": {"gv": 1, "e2": 18, "ke": 23.7, "e4": 25.7, "kd": 29.2, "e8": 37.2, "e16": 41.6,
                        "e32": 52.3, "e64": 62.5, "qd": 66.5, "sl": 66.6},
                     "pe": {"dec": 1, "kk": 2.3, "xt1": 14.8, "tt2": 16.7, "ks": 18.7, "pt2": 20.3, "px2": 22.9,
                        "tt4": 24.1, "pt4": 29.1, "px4": 30, "tt8": 32.2, "px8": 32.7, "pt8": 32.8, "tt16": 36.9,
                        "pt16": 42.1, "px16": 42.3, "tt32": 46, "pt32": 49.3, "px32": 49.9, "tt64": 52.7,
                        "px64": 59.2, "w": 61.3, "o": 65.7, "ds": 67.7}}

            def __init__(self, name, before, meta):
                super().__init__(name, before)
                self.meta = meta
                self.n = META if meta else CH
                self.levels = [b for b in LEVELS[1:] if b < self.n]
                self.last = self.levels[-1]
                self.groups = [[(0, 0)], [(0, 1)]] if meta else [[(0, 0), (0, 1)], [(1, 0), (1, 1)]]
                self.ng = len(self.groups[0])
                if meta:
                    L = self.levels
                    order = {"act": ["gc", "bc", "kc", "dec", "xt1"] + [f"tt{b}" for b in L],
                             "pool": ["gv", "e2"] + [f"e{b}" for b in L[1:]] + ["kd"],
                             "pe": ["kk", "dec", "xt1"] + [n_ + str(b) for b in L for n_ in ("tt", "pt", "px") if n_ != "pt" or b != L[-1]] + ["w", "ds"],
                             "dve": ["a", "e1", "x1"] + [n_ + str(b) for b in L for n_ in ("xt", "x") if n_ != "xt" or b != L[-1]] + ["vn", "s"]}
                    ph = [(eng, n_, float(t)) for eng, names in order.items() for t, n_ in enumerate(names)]
                else:
                    ph = [(eng, n_, t) for eng, names in self.TIMES.items() for n_, t in names.items()]
                self.iters = 1 if meta else NCH
                window = self.ng * self.PERIOD
                lag = 0.01 if meta else self.SHIFT
                self.events = {}
                for eng in ("act", "dve", "pool", "pe"):
                    ev = []
                    for s in range(2):
                        names = []
                        for g in range(self.ng):
                            for q, n_, t in sorted([p_ for p_ in ph if p_[0] == eng], key=lambda p_: p_[2]):
                                at_ = g * self.PERIOD + t + s * lag
                                late = int(at_ >= window)
                                names.append((n_, g))
                                ev.append((at_ - late * window, late, s, g, n_))
                        st_ = Steps(sem(f"s_{name}_{eng}{s}"), names)
                        st_.iters = self.iters
                        self.log[eng, s] = st_
                    self.events[eng] = sorted(ev)

            def each(self, e, eng, fns):
                self.begin(e, eng)

                def some(it, lates):
                    for _, late, s, g, name in self.events[eng]:
                        if late in lates:
                            d, half = self.groups[s][g]
                            self.asked = {}
                            n = it - 1 if late else it
                            self.did((eng, s), fns(name, n, g, s, d, half), (name, g))
                if self.meta:
                    some(0, (0,))
                    return
                some(0, (0,))
                with e.Fori(1, NCH) as it:
                    some(it, (0, 1))
                some(NCH, (1,))

            def w(self, e, it, g, s, eng, name, before=False):
                if not before:
                    self.ask((eng, s), (name, g), 0)
                elif g:
                    self.ask((eng, s), (name, g - 1), 0)
                else:
                    self.ask((eng, s), (name, self.ng - 1), 1)

            def ask(self, key, step, back):
                n = self.log[key].count(0, step, back)
                if n > self.asked.get(key, (0,))[0]:
                    self.asked[key] = (n, step, back)

            def flush(self, e, it):
                for key, (_, step, back) in self.asked.items():
                    self.on(e, key, it, step, back)
                self.asked = {}

            def state(self, g, s):
                self.ask(("dve", s), ("s", g), 1)

            def chunk(self, it, d):
                if self.meta:
                    return 0, 0
                c = it if d == 0 else it * -1 + (NCH - 1)
                return c + 1, c

            def wt(self, name, s):
                return work[name][0:self.n, s, :, 0:self.n]

            def bank(self, s, b, rows, cols):
                return ps[0:rows, 4 * s + b, 0:HG * cols].rearrange("p (u m) -> p u m", u=HG)

            def cols(self, t, b, parity):
                return t.rearrange("p u (n two b) -> p u two n b", two=2, b=b)[:, :, parity]

            def packed(self, s, bank, b):
                return self.bank(s, bank, self.n, self.n // 2).rearrange("p u (n b) -> p u n b", b=b)

            def toks(self, t, it, d, half):
                if self.meta:
                    return t[:, half * HG:(half + 1) * HG, 0:META]
                c = self.chunk(it, d)[1]
                return t[:, half * HG:(half + 1) * HG, bass.ds(c * CH + META, CH)]

            def cell(self, tab, it, d, half):
                h0 = d * H + half * HG
                return tab[0:self.n, self.chunk(it, d)[0], h0:h0 + HG]

            def col(self, tab, it, d, half, width, rows=None):
                c = self.chunk(it, d)[0]
                h0 = d * H + half * HG
                return tab[0:(rows or self.n), c, h0:h0 + HG].unsqueeze(2).to_broadcast([rows or self.n, HG, width])

            def act(self, e):
                n = self.n

                def f(name, it, g, s, d, half):
                    w = lambda *q: self.w(e, it, g, s, *q)
                    if name == "gc":
                        w("pe", "dec", True)
                        self.flush(e, it)
                        return e.activation(g_now[0:n, s, :], self.cell(gdec, it, d, half), ACT.Copy)
                    if name == "bc":
                        w("dve", "a", True)
                        self.flush(e, it)
                        return e.activation(b_now[0:n, s, :], self.cell(beta, it, d, half), ACT.Copy)
                    if name == "kc":
                        w("pe", "kk", True)
                        if not self.meta:
                            w("pe", "ks", True)
                            w("pool", "ke", True)
                        self.flush(e, it)
                        return e.activation(work["kc"][:, s, :, 0:n], self.toks(kT, it, d, half), ACT.Copy)
                    if name == "dec":
                        w("pe", "dec")
                        if not self.meta:
                            w("pe", "o", True)
                        self.flush(e, it)
                        return e.activation(self.wt("dec", s), self.bank(s, 0, n, n), ACT.Exp)
                    if name == "eg":
                        w("pe", "dec")
                        w("dve", "s", True)
                        self.flush(e, it)
                        return e.activation(work["eg"][:, s, :, :], self.bank(s, 1, P, n), ACT.Exp)
                    if name == "xt1":
                        w("pe", "xt1")
                        if not self.meta:
                            w("pe", "o", True)
                        self.flush(e, it)
                        return e.activation(self.wt("xt", s), self.bank(s, 0, n, n), ACT.Copy)
                    w("pe", name)
                    self.flush(e, it)
                    return e.activation(self.wt("tt", s), self.bank(s, 1, n, n), ACT.Copy)
                self.each(e, "act", f)

            def pool(self, e):
                n = self.n

                def f(name, it, g, s, d, half):
                    w = lambda *q: self.w(e, it, g, s, *q)
                    A, E = self.wt("a", s), self.wt("e", s)
                    if name == "gv":
                        w("act", "gc")
                        w("pe", f"tt{self.last}", True)
                        gb = g_now[0:n, s, :].unsqueeze(2).to_broadcast([n, HG, n])
                        v = cmat("vb" if d else "vf")[0:n, 0:n].unsqueeze(1).to_broadcast([n, HG, n])
                        self.flush(e, it)
                        return e.tensor_tensor(E, v, gb, ALU.mult)
                    if name[0] == "e":
                        b = int(name[1:])
                        w("pe", f"tt{b // 2}" if b > 2 else "dec")
                        w("dve", "a")
                        m = cmat("m" + name[1:])[0:n, 0:n].unsqueeze(1).to_broadcast([n, HG, n])
                        self.flush(e, it)
                        return e.tensor_tensor(E, A, m, ALU.mult)
                    if name == "ke":
                        w("act", "eg")
                        w("pe", "kk")
                        self.flush(e, it)
                        return e.tensor_tensor(work["kc"][:, s], work["kc"][:, s], work["eg"][:, s], ALU.mult)
                    if name == "kd":
                        if self.meta:
                            w("pool", f"e{self.last}")
                            src, dst = k_met[0:n, half * HG:(half + 1) * HG, :], work["a"]
                        else:
                            w("pe", "ds", True)
                            src, dst = k_tok[:, self.chunk(it, d)[1], half * HG:(half + 1) * HG, :], work["kd"]
                        self.flush(e, it)
                        return e.tensor_tensor(dst[0:n, s], src, self.col(kcol, it, d, half, P), ALU.mult)
                    if name == "qd":
                        w("pe", f"tt{self.last}")
                        w("act", "eg")
                        self.flush(e, it)
                        return e.tensor_tensor(work["xt"][:, s], self.toks(qT, it, d, half), work["eg"][:, s], ALU.mult)
                    if name == "sl":
                        w("pool", "qd")
                        self.state(g, s)
                        S = st[:, d, half * HG:(half + 1) * HG, :]
                        self.flush(e, it)
                        return e.tensor_tensor(work["eg"][:, s], S, self.col(lcol, it, d, half, P, P), ALU.mult)
                self.each(e, "pool", f)

            def pe(self, e):
                n = self.n
                I4 = range(HG)

                def f(name, it, g, s, d, half):
                    w = lambda *q: self.w(e, it, g, s, *q)
                    bk = lambda b, rows, cols: self.bank(s, b, rows, cols)
                    E, X, XT, TT = self.wt("e", s), self.wt("x", s), self.wt("xt", s), self.wt("tt", s)
                    S = st[:, d, half * HG:(half + 1) * HG, :]
                    kc = work["kc"]
                    if name == "kk":
                        w("act", "kc")
                        w("dve", "s", True)
                        if not self.meta:
                            w("dve", "o", True)
                        self.flush(e, it)
                        for u in I4:
                            m = e.matmul(bk(2, n, n)[:, u], kc[:, s, u, 0:n], kc[:, s, u, 0:n], start=True, stop=True)
                            if not self.meta:
                                c = self.chunk(it, d)[1]
                                m = e.matmul(bk(3, n, n)[:, u], kc[:, s, u, 0:n], qT[:, half * HG + u, bass.ds(c * CH + META, CH)], start=True, stop=True)
                        return m
                    if name == "dec":
                        w("pool", "gv")
                        w("dve", "vn", True)
                        U = cmat("ub" if d else "uf")
                        self.flush(e, it)
                        for u in I4:
                            e.matmul(bk(0, n, n)[:, u], E[:, u], U[0:n, 0:n], start=True, stop=False)
                            m = e.matmul(bk(0, n, n)[:, u], cb[0:n, 0, 0:n], cb[0:n, 1 + d, 0:n], start=False, stop=True)
                        if not self.meta:
                            for u in I4:
                                m = e.matmul(bk(1, P, n)[:, u], g_now[:, s, u:u + 1].to_broadcast([P, P]), U, start=True, stop=True)
                        return m
                    if name == "xt1":
                        w("dve", "x1")
                        w("act", "dec")
                        self.flush(e, it)
                        for u in I4:
                            m = e.transpose(bk(0, n, n)[:, u], X[:, u], cmat("ident")[0:n, 0:n])
                        return m
                    if name[:2] == "tt":
                        b = int(name[2:])
                        w("pool", f"e{b}")
                        if b == 2:
                            w("act", "xt1")
                            if not self.meta:
                                w("act", "eg")
                        else:
                            w("dve", f"xt{b // 2}")
                            w("act", f"tt{b // 2}")
                        self.flush(e, it)
                        for u in I4:
                            m = e.matmul(bk(1, n, n)[:, u], E[:, u], XT[:, u], start=True, stop=True)
                        return m
                    if name[:2] == "pt":
                        b = int(name[2:])
                        w("act", f"tt{b}")
                        w("dve", "x1" if b == 2 else f"x{b // 2}")
                        if b == 2 and not self.meta:
                            w("dve", "qk")
                        self.flush(e, it)
                        for u in I4:
                            m = e.matmul(self.packed(s, 3, b)[:, u], X[:, u], self.cols(TT, b, d)[:, u], start=True, stop=True)
                        return m
                    if name[:2] == "px":
                        b = int(name[2:])
                        w("act", f"tt{b}")
                        w("dve", "x1" if b == 2 else f"x{b // 2}")
                        self.flush(e, it)
                        for u in I4:
                            m = e.matmul(self.packed(s, 2, b)[:, u], TT[:, u], self.cols(X, b, 1 - d)[:, u], start=True, stop=True)
                        return m
                    if name == "ks":
                        w("pool", "ke")
                        w("act", "xt1")
                        self.state(g, s)
                        self.flush(e, it)
                        for u in I4:
                            m = e.matmul(bk(0, n, P)[:, u], kc[:, s, u, :], S[:, u], start=True, stop=True)
                        return m
                    if name == "w":
                        w("dve", f"x{self.last}")
                        w("act", f"tt{self.last}")
                        if not self.meta:
                            w("dve", "r")
                        self.flush(e, it)
                        for u in I4:
                            r = v_met[0:n, half * HG + u, :] if self.meta else work["r"][:, s, u, :]
                            m = e.matmul(bk(1, n, P)[:, u], X[:, u], r, start=True, stop=True)
                        return m
                    if name == "ds":
                        w("pool", "kd")
                        w("dve", "vn")
                        kd = work["a" if self.meta else "kd"]
                        self.flush(e, it)
                        for u in I4:
                            m = e.matmul(bk(3, P, P)[:, u], kd[0:n, s, u, :], work["tt"][0:n, s, u, :], start=True, stop=True)
                        return m
                    if name == "o":
                        w("pool", "qd")
                        w("dve", "vn")
                        self.state(g, s)
                        self.flush(e, it)
                        for u in I4:
                            e.matmul(bk(2, P, n)[:, u], S[:, u], work["xt"][:, s, u, :], start=True, stop=False)
                            m = e.matmul(bk(2, P, n)[:, u], work["tt"][:, s, u, :], work["dec"][:, s, u, :], start=False, stop=True)
                        return m
                self.each(e, "pe", f)

            def dve(self, e):
                n = self.n

                def f(name, it, g, s, d, half):
                    w = lambda *q: self.w(e, it, g, s, *q)
                    bk = lambda b, rows, cols: self.bank(s, b, rows, cols)
                    X, XT = self.wt("x", s), self.wt("xt", s)
                    S = st[:, d, half * HG:(half + 1) * HG, :]
                    if name == "a":
                        w("pe", "kk")
                        w("act", "dec")
                        w("act", "bc")
                        w("pool", f"e{self.last}", True)
                        self.flush(e, it)
                        for u in range(HG):
                            m = e.scalar_tensor_tensor(self.wt("a", s)[:, u], bk(2, n, n)[:, u], b_now[0:n, s, u:u + 1],
                                                       self.wt("dec", s)[:, u], ALU.mult, ALU.mult)
                        return m
                    if name == "e1":
                        w("dve", "a")
                        w("pe", "w", True)
                        m = cmat("m1")[0:n, 0:n].unsqueeze(1).to_broadcast([n, HG, n])
                        self.flush(e, it)
                        return e.tensor_tensor(X, self.wt("a", s), m, ALU.mult)
                    if name == "x1":
                        w("dve", "e1")
                        i = cmat("ident")[0:n, 0:n].unsqueeze(1).to_broadcast([n, HG, n])
                        self.flush(e, it)
                        return e.tensor_tensor(X, i, X, ALU.subtract)
                    if name == "qk":
                        w("dve", "a")
                        self.flush(e, it)
                        return e.tensor_tensor(self.wt("dec", s), bk(3, n, n), self.wt("dec", s), ALU.mult)
                    if name == "r":
                        w("pe", "ks")
                        w("pe", "w", True)
                        v = v_tok[:, self.chunk(it, d)[1], half * HG:(half + 1) * HG, :]
                        self.flush(e, it)
                        return e.tensor_tensor(work["r"][:, s], v, bk(0, n, P), ALU.subtract)
                    if name == "vn":
                        w("pe", "w")
                        self.flush(e, it)
                        return e.tensor_tensor(work["tt"][0:n, s], bk(1, n, P), self.col(beta, it, d, half, P), ALU.mult)
                    if name == "s":
                        w("pe", "ds")
                        if self.meta:
                            self.flush(e, it)
                            return e.tensor_copy(S, bk(3, P, P))
                        w("pool", "sl")
                        w("pe", "o")
                        self.flush(e, it)
                        return e.tensor_tensor(S, work["eg"][:, s], bk(3, P, P), ALU.add)
                    if name == "o":
                        w("pe", "o")
                        w("dve", "o", True)
                        self.w(e, it, g, 1 - s, "dve", "o", True)
                        o = oT[:, half * HG:(half + 1) * HG, bass.ds(self.chunk(it, d)[1] * CH, CH)]
                        self.flush(e, it)
                        return e.tensor_tensor(o, o, bk(2, P, n), ALU.add)
                    if name[:2] == "xt":
                        b = int(name[2:])
                        w("pe", f"pt{b}")
                        w("act", "xt1") if b == 2 else w("dve", f"xt{b // 2}")
                        v = self.cols(XT, b, d)
                        self.flush(e, it)
                        return e.tensor_tensor(v, v, self.packed(s, 3, b), ALU.subtract)
                    b = int(name[1:])
                    w("pe", f"px{b}")
                    w("dve", "x1" if b == 2 else f"x{b // 2}")
                    v = self.cols(X, b, 1 - d)
                    self.flush(e, it)
                    return e.tensor_tensor(v, v, self.packed(s, 2, b), ALU.subtract)
                self.each(e, "dve", f)

        zeroed = [0]

        def zero(e, *aps):
            for ap in aps:
                e.memset(ap, 0.0).then_inc(s_zero, 1)
            zeroed[0] += len(aps)
            e.wait_ge(s_zero, zeroed[0])

        TOK = ((META, T1),)
        ALL = ((0, SEQ),)

        def split(dst_hi, dst_lo, val, done, tile=lambda i: i):
            return [("act", "hi", [("dve", done, 0)], lambda e, i, j: e.activation(dst_hi[:, tile(i), :], row(val + j % 2), ACT.Copy), 1),
                    ("pool", "lo", [("act", "hi", 0)], lambda e, i, j: e.tensor_tensor(
                        dst_lo[:, tile(i), :], row(val + j % 2), dst_hi[:, tile(i), :].bitcast(F32), ALU.subtract), 1)]

        def one(b0):
            return lambda j, o: [ps[:, b0 + j % 4, :]]

        def gate_z(before):
            return Linear("z", before, H // 8, 8, [(0, h_hi, h_lo, K8, True, True)], one(0), {0: ("act", "silu", 4)}, [
                ("act", "prert", [("pe", "ss", 0), ("dve", "n", 2)], lambda e, i, j: e.activation(row(4 + j % 2), ps[:, 4, :], ACT.Sqrt, bias=eps_col), 1),
                ("act", "presq", [("pe", "ss", 2)], lambda e, i, j: e.activation(row(j % 2), oT[:, i, :], ACT.Square)),
                ("pe", "ss", [("act", "presq", 0), ("act", "prert", 1)], lambda e, i, j: e.matmul(ps[:, 4, :], cmat("mean128"), row(j % 2), start=True, stop=True)),
                ("dve", "rec", [("act", "prert", 0)], lambda e, i, j: e.reciprocal(row(4 + j % 2), row(4 + j % 2)), 1),
                ("dve", "n", [("dve", "rec", 0)], lambda e, i, j: e.scalar_tensor_tensor(
                    oT[:, i, :], oT[:, i, :], pcol("dnn", 0), row(4 + j % 2), ALU.mult, ALU.mult), 1),
                ("dve", "v", [("dve", "n", 0), ("act", "silu", 0)], lambda e, i, j: e.tensor_tensor(zs[:, i, :], zs[:, i, :], oT[:, i, :], ALU.mult), 1),
                ("act", "silu", [("out", 0)], lambda e, i, j: e.activation(zs[:, i, :], ps[:, j % 4, :], ACT.Silu)),
                ("act", "hi", [("dve", "v", 0)], lambda e, i, j: e.activation(od_hi[:, i, :], zs[:, i, :], ACT.Copy), 2),
                ("pool", "lo", [("act", "hi", 0)], lambda e, i, j: e.tensor_tensor(
                    od_lo[:, i, :], zs[:, i, :], od_hi[:, i, :].bitcast(F32), ALU.subtract), 2),
            ], width=TOK)

        CW = SEQ + 4
        def short_conv(before):
            wide = ((META - 4, META - 4 + CW // 2), (META - 4 + CW // 2, T1))
            bank = lambda j, o: ([ps[:, 2 * o, 0:CW // 2], ps[:, 2 * o + 1, 0:CW // 2]] if o < 2 else [ps[:, 4 + j % 2, :]])

            def tap(t):
                if t == 0:
                    return ("dve", "c0", [("dve", "cx", 0), ("pool", "lo", 2)], lambda e, i, j: e.tensor_scalar(
                        row(4 + j % 2), row(1, SEQ, 3), pcol("sc", i), None, ALU.mult))
                return ("dve", f"c{t}", [("dve", f"c{t - 1}", 0)], lambda e, i, j: e.scalar_tensor_tensor(
                    row(4 + j % 2), row(1, SEQ, 3 + t), pcol("sc", i, t), row(4 + j % 2), ALU.mult, ALU.add))
            return Linear("sc", before, KT // 4, 4, [(o, h_hi, h_lo, K8, True, True) for o in range(3)], bank,
                          {0: ("act", "c", 1), 1: ("dve", "cx", 1), 2: ("dve", "v", 2)}, [
                ("act", "c", [("out", 0), ("dve", "cx", 1)], lambda e, i, j: e.activation(pair(row(0, CW)), ps[:, 0:2, 0:CW // 2], ACT.Copy)),
                ("dve", "cx", [("out", 1), ("act", "c", 0), ("dve", "c2", 1)], lambda e, i, j: e.tensor_tensor(
                    pair(row(1, CW)), ps[:, 2:4, 0:CW // 2], pair(row(0, CW)), ALU.mult)),
                tap(0), tap(1), tap(2),
                ("dve", "v", [("out", 2), ("dve", "c2", 0)], lambda e, i, j: e.tensor_tensor(row(4 + j % 2), row(4 + j % 2), ps[:, 4 + j % 2, :], ALU.mult)),
            ] + split(sc_hi, sc_lo, 4, "v"), width={0: wide, 1: wide, 2: TOK}, after=before,
                start={"dve": lambda e: zero(e, row(1, 4, CW))})

        def two_banks(j, o):
            return [ps[:, 2 * (j % 2) + o, :]]

        def branch_sc(before):
            return Linear("bsc", before, KT // 2, 2, [(0, h_hi, h_lo, K8, True, True), (1, sc_hi, sc_lo, K8, True, True)], two_banks,
                          {0: ("act", "sg", 2), 1: ("dve", "v", 2)}, [
                ("act", "sg", [("out", 0), ("dve", "v", 2)], lambda e, i, j: e.activation(row(j % 2), ps[:, 2 * (j % 2), :], ACT.Sigmoid)),
                ("dve", "v", [("out", 1), ("act", "sg", 0)], lambda e, i, j: e.tensor_tensor(m1[:, i, :], row(j % 2), ps[:, 2 * (j % 2) + 1, :], ALU.mult)),
            ], width={0: TOK, 1: ALL}, after=before, feed=[(sc_hi, from_items(before))])

        def branch_dn(before):
            return Linear("bdn", before, KT // 2, 2, [(0, h_hi, h_lo, K8, True, True), (1, od_hi, od_lo, K8, True, True)], two_banks,
                          {0: ("act", "sg", 2), 1: ("dve", "t", 2)}, [
                ("act", "sg", [("out", 0), ("dve", "t", 2)], lambda e, i, j: e.activation(row(j % 2), ps[:, 2 * (j % 2), :], ACT.Sigmoid)),
                ("dve", "t", [("out", 1), ("act", "sg", 0), ("pool", "lo", 2)], lambda e, i, j: e.tensor_tensor(
                    row(2 + j % 2), row(j % 2), ps[:, 2 * (j % 2) + 1, :], ALU.mult)),
                ("dve", "v", [("dve", "t", 0)], lambda e, i, j: e.tensor_tensor(row(2 + j % 2), row(2 + j % 2), m1[:, i, :], ALU.add)),
            ] + split(me_hi, me_lo, 2, "v"), width={0: TOK, 1: ALL}, after=before,
                start={"act": lambda e: e.dma_start(x_res[:], a["x"][:, :, META:T1]).then_inc(s_xr, 16)})

        def residual(name, before, hi, lo, parts, made, made_by=None, first=None, w0=None):
            n, m = len(parts), 4
            units, k = [], 0
            for p_, c in enumerate(parts):
                units.append((0, hi, lo, [(t, k + t) for t in range(c)], p_ == 0, p_ == n - 1))
                k += c
            src = x if first is None else first

            def sums(tag, acc, r, scale):
                def sq(e, i, j):
                    return e.activation(row(acc if i == 0 else r + j % 2), x[:, i, :], ACT.Square, scale=scale(i))

                def add(e, i, j):
                    if i == 0:
                        return e.memset(row(r, 1), 0.0)
                    return e.tensor_tensor(row(acc), row(acc), row(r + j % 2), ALU.add)
                return [("act", "sq" + tag, [("dve", "v", 0), ("dve", "acc" + tag, 2)], sq),
                        ("dve", "acc" + tag, [("act", "sq" + tag, 0), ("dve", "acc" + tag, 1)], add, 1)]
            after = sums("", 4, 2, lambda i: 1.0) + (sums("0", 7, 5, lambda i: pcol(w0, i)) if w0 else [])
            return Linear(name, before, KT // m, m, units, one(0), {0: ("dve", "v", 4)}, [
                ("dve", "v", [("out", 0)], lambda e, i, j: e.tensor_tensor(x[:, i, :], src[:, i, :], ps[:, j % 4, :], ALU.add)),
            ] + after, width=ALL, final=True, after=made, feed=[(hi, made_by or from_items(made))], start={"dve": lambda e: e.wait_ge(s_xr, 16)})

        def gate_up(before):
            return Linear("gu", before, FT // 2, 2, [(0, h_hi, h_lo, K8, True, True), (1, h_hi, h_lo, K8, True, True)], two_banks,
                          {0: ("act", "sg", 2), 1: ("dve", "v", 2)}, [
                ("act", "sg", [("out", 0), ("dve", "v", 2)], lambda e, i, j: e.activation(row(j % 2), ps[:, 2 * (j % 2), :], ACT.Silu)),
                ("dve", "v", [("out", 1), ("act", "sg", 0), ("pool", "lo", 2)], lambda e, i, j: e.tensor_tensor(
                    row(2 + j % 2), row(j % 2), ps[:, 2 * (j % 2) + 1, :], ALU.mult)),
            ] + split(y_hi, y_lo, 2, "v"), width=TOK, after=before, feed=[(h_hi, from_norm(before))])

        TAPS = PAR["ca"][2]

        def conv_step(e, k, t):
            if t == TAPS:
                return e.tensor_tensor(uc[:, k, 1:SEQ], uc[:, k, 1:SEQ], row(7)[:, 1:SEQ], ALU.add)
            w = pcol("ca", k, TAPS - 1 - t)
            acc = row(7) if t % 2 else uc[:, k, :]
            if t == 0:
                return e.tensor_scalar(acc, u_in[:, k, :], w, pcol("cab", k), ALU.mult, ALU.add)
            if t == 1:
                return e.tensor_scalar(acc[:, 1:SEQ], u_in[:, k, 0:SEQ - 1], w, None, ALU.mult)
            return e.scalar_tensor_tensor(acc[:, t:SEQ], u_in[:, k, 0:SEQ - t], w, acc[:, t:SEQ], ALU.mult, ALU.add)

        STEPS = TAPS + 1

        def conv_part(stage, tile, items, first):
            n = STEPS // items

            def step(c):
                waits = [("dve", f"cv{c - 1 if c == n - 1 else c - 2}", 0)] if c > 1 else first
                return ("dve", f"cv{c}", waits, lambda e, i, j: conv_step(e, tile(stage[0].it, j), (j % items) * n + c))
            return [step(c) for c in range(n)]

        def glu_conv(before):
            me = []
            me.append(Linear("glu", before, KT // 2, 2, [(0, h_hi, h_lo, K8, True, True), (1, h_hi, h_lo, K8, True, True)], two_banks,
                          {0: ("dve", "u", 2), 1: ("act", "sg", 2)}, [
                ("act", "sg", [("out", 1), ("dve", "u", 2)], lambda e, i, j: e.activation(row(j % 2), ps[:, 2 * (j % 2) + 1, :], ACT.Sigmoid)),
                ("dve", "u", [("out", 0), ("act", "sg", 0)], lambda e, i, j: e.tensor_tensor(
                    u_in[:, i, :], row(j % 2), ps[:, 2 * (j % 2), :], ALU.mult)),
            ] + conv_part(me, lambda it, j: it, 2, [("dve", "u", 0)]), width=TOK, after=before, feed=[(h_hi, from_norm(before))]))
            return me[0]

        PART = 5

        class PoolDiff(Linear):

            def __init__(self, before):
                self.off = 16
                super().__init__("bval", before, 1, KT, [(0, h_hi, h_lo, K8, True, True)], one(0), {0: ("act", "bv", 4)}, [], width=TOK, after=before)
                names = []
                self.conv = [(k, t) for k in (4, 5) for t in range(STEPS)][:KT * PART]
                for j in range(KT):
                    names += [("s", j, n) for n in range(j // 2 + 1)] + [("d", j), ("q", j), ("f", j)]
                    names += [("cv", *q) for q in self.conv[j * PART:(j + 1) * PART]]
                self.steps("dve", names)
                self.steps("pool", [("lo", j) for j in range(KT)])
                self.steps("act", [(n_, j) for j in range(KT) for n_ in ("bv", "hi")])

            def psum_read(self, e):
                self.on(e, "act", 0, ("bv", KT - 1))

            def act(self, e):
                self.before.wait_whole(e, ("act", "pool"))
                self.before.on(e, "dve", self.before.n - 1, ("u", self.before.m - 1))
                for j in range(KT):
                    c = j + 2
                    round_unit(e, BASE["bval"] + c, c)
                    e.wait_ge(s_pe, BASE["bval"] + j + 1)
                    if j > 1:
                        self.on(e, "dve", 0, ("f", j - 2))
                    self.did("act", e.activation(row(j % 2, SEQ, 16), ps[:, j % 4, :], ACT.Copy), ("bv", j))
                    self.on(e, "dve", 0, ("f", j))
                    self.did("act", e.activation(mx_hi[:, KT + j, :], row(4 + j % 2), ACT.Copy), ("hi", j))

            def pool(self, e):
                self.before.wait_whole(e, ("act", "pool"))
                for j in range(KT):
                    split_unit(e, BASE["bval"] + j + 2, j + 2)
                    self.on(e, "act", 0, ("hi", j))
                    self.did("pool", e.tensor_tensor(mx_lo[:, KT + j, :], row(4 + j % 2), mx_hi[:, KT + j, :].bitcast(F32), ALU.subtract), ("lo", j))

            def dve(self, e):
                self.begin(e, "dve")
                zero(e, *[row(r, 16) for r in range(4)])
                for j in range(KT):
                    w = POOLW[j // 2]
                    self.on(e, "act", 0, ("bv", j))
                    last = ("f", j - 1)
                    src = j % 2
                    for n in range(j // 2 + 1):
                        if last[1] >= 0:
                            self.on(e, "dve", 0, last)
                        dst = 2 + n % 2
                        self.did("dve", e.tensor_tensor(row(dst, SEQ, 16), row(src, SEQ, 16), row(src, SEQ, 16 - 2 ** n), ALU.add), ("s", j, n))
                        last, src = ("s", j, n), dst
                    self.on(e, "dve", 0, last)
                    if j > 1:
                        self.on(e, "pool", 0, ("lo", j - 2))
                    v = row(4 + j % 2)
                    self.did("dve", e.scalar_tensor_tensor(v, row(src, SEQ, 16), 1.0 / w, row(j % 2, SEQ, 16), ALU.mult, ALU.subtract), ("d", j))
                    cnt = small[:, 48 + 16 * (j // 2):64 + 16 * (j // 2)]
                    self.did("dve", e.tensor_tensor(row(6, 16), row(src, 16, 16), cnt, ALU.mult), ("q", j))
                    self.on(e, "dve", 0, ("q", j))
                    self.did("dve", e.tensor_tensor(v[:, 0:16], row(6, 16), row(j % 2, 16, 16), ALU.subtract), ("f", j))
                    for k, t in self.conv[j * PART:(j + 1) * PART]:
                        if t == 0:
                            self.on(e, "dve", 0, ("f", j))
                        elif t == 1 or t == TAPS or (k, t - 2) not in self.conv[j * PART:(j + 1) * PART]:
                            self.on(e, "dve", 0, ("cv", k, t - 1))
                        else:
                            self.on(e, "dve", 0, ("cv", k, t - 2))
                        self.did("dve", conv_step(e, k, t), ("cv", k, t))

        def pool_mix(before):
            def emit(o):
                return lambda e, i, j: e.tensor_scalar(yb[:, i * 2 + o, :], ps[:, 2 * (j % 2) + o, :], pcol("pb", i * 2 + o), pcol("psc", i * 2 + o), ALU.add, ALU.mult)
            tiles = [[(2 * o + k, lambda j, k=k: KT + 2 * j + k) for k in range(2)] for o in range(2)]
            rest = [(k, t) for k in (4, 5) for t in range(STEPS)][KT * PART:]
            n = len(rest) // 4

            def conv(c):
                def step(e, i, j):
                    return conv_step(e, *rest[j * n + c])
                return ("dve", f"cv{c}", [("dve", f"cv{c - 1 if c == n - 1 else c - 2}" if c > 1 else "v1", 0)], step)
            return Linear("pool", before, 1, 4, [(0, mx_hi, mx_lo, tiles, True, True)],
                          lambda j, o: [[ps[:, 2 * (j % 2), :]], [ps[:, 2 * (j % 2) + 1, :]]], {0: ("dve", "v1", 2)}, [
                ("dve", "v0", [("out", 0)], emit(0)),
                ("dve", "v1", [("out", 0)], emit(1)),
            ] + [conv(c) for c in range(n)], width=ALL, after=before, feed=[(mx_hi, lambda k: (before, 0, ("lo", k - KT)))])

        def a_gate(before):
            me = []
            me.append(Linear("agate", before, KT // 4, 4, [(0, h_hi, h_lo, K8, True, True)], one(0), {0: ("act", "sg", 4)}, [
                ("act", "sg", [("out", 0)], lambda e, i, j: e.activation(sg_a[:, i, :], ps[:, j % 4, :], ACT.Silu)),
            ] + conv_part(me, lambda it, j: it + 6, 4, [("dve", "cv7", 1)]), width=TOK, after=before))
            return me[0]

        def b_gate(before):
            whole = list(range(KT))
            norm, after = {3: [0, 1], 4: [2, 3], 5: [4, 5], 6: [6, 7]}, {4: [0, 1], 5: [2, 3], 6: [4, 5], 7: [6, 7]}
            return Linear("bgate", before, 1, KT, [(0, h_hi, h_lo, K8, True, True)], one(0), {0: ("act", "sg", 4)}, [
                ("act", "sg", [("out", 0), ("dve", "v", 2)], lambda e, i, j: e.activation(row(j % 2), ps[:, j % 4, :], ACT.Silu)),
                ("dve", "v", [("act", "sg", 0), ("pool", "lo", 2)], lambda e, i, j: e.tensor_tensor(row(2 + j % 2), row(j % 2), yb[:, i, :], ALU.mult)),
            ] + split(mx_hi, mx_lo, 2, "v", lambda i: i + KT) + [
                ("dve", "su", [("dve", "su", 1)], lambda e, i, j: (
                    e.tensor_copy(row(6), uc[:, 0, :]) if j == 0 else e.tensor_tensor(row(6), row(6), uc[:, j, :], ALU.add)), {0: whole}),
                ("pe", "mu", [("dve", "su", "#7")], lambda e, i, j: e.matmul(ps[:, 4, :], cmat("mean1024"), row(6), start=True, stop=True), {1: [0]}),
                ("dve", "mu", [("pe", "mu", "#0")], lambda e, i, j: e.tensor_copy(row(6), ps[:, 4, :]), {1: [0]}),
                ("dve", "c", [("dve", "mu", "#0")], lambda e, i, j: e.tensor_tensor(uc[:, j, :], uc[:, j, :], row(6), ALU.subtract), {1: whole}),
                ("act", "sq", [("dve", "c", 0), ("dve", "sv", 2)], lambda e, i, j: e.activation(row(4 + j % 2), uc[:, j, :], ACT.Square), {1: whole}),
                ("dve", "sv", [("act", "sq", 0), ("dve", "sv", 1)], lambda e, i, j: (
                    e.tensor_copy(row(7), row(4)) if j == 0 else e.tensor_tensor(row(7), row(7), row(4 + j % 2), ALU.add)), {1: whole}),
                ("pe", "ss", [("dve", "sv", "#7")], lambda e, i, j: e.matmul(ps[:, 5, :], cmat("mean1024"), row(7), start=True, stop=True), {2: [0]}),
                ("act", "rt", [("pe", "ss", "#0")], lambda e, i, j: e.activation(row(7), ps[:, 5, :], ACT.Sqrt, bias=small[:, 126:127]), {2: [0]}),
                ("dve", "rec", [("act", "rt", "#0")], lambda e, i, j: e.reciprocal(row(7), row(7)), {2: [0]}),
                ("dve", "n", [("dve", "rec", "#0")], lambda e, i, j: e.tensor_tensor(uc[:, j, :], uc[:, j, :], row(7), ALU.mult), norm),
                ("act", "u", [("dve", "n", 0)], lambda e, i, j: e.activation(uc[:, j, :], uc[:, j, :], ACT.Silu, bias=pcol("lnb", j), scale=pcol("lng", j)), norm),
                ("dve", "a", [("act", "u", 0), ("pool", "alo", 2)], lambda e, i, j: e.tensor_tensor(row(4 + j % 2), uc[:, j, :], sg_a[:, j, :], ALU.mult), after),
                ("act", "ahi", [("dve", "a", 0)], lambda e, i, j: e.activation(mx_hi[:, j, :], row(4 + j % 2), ACT.Copy), after),
                ("pool", "alo", [("act", "ahi", 0)], lambda e, i, j: e.tensor_tensor(
                    mx_lo[:, j, :], row(4 + j % 2), mx_hi[:, j, :].bitcast(F32), ALU.subtract), after),
            ], width=TOK, after=before)

        def lru_conv(before):
            def tap(t):
                if t == 0:
                    return ("dve", "c0", [("act", "evac", 0)], lambda e, i, j: e.tensor_scalar(
                        xc[:, i, :], row(j % 2), pcol("cc", i), pcol("ccb", i), ALU.mult, ALU.add))
                return ("dve", f"c{t}", [("dve", f"c{t - 1}", 0)], lambda e, i, j: e.scalar_tensor_tensor(
                    xc[:, i, :], row(j % 2, SEQ, t), pcol("cc", i, t), xc[:, i, :], ALU.mult, ALU.add))
            return Linear("xr", before, LT // 4, 4, [(0, h_hi, h_lo, K8, True, True)], one(0), {0: ("act", "evac", 4)}, [
                ("act", "evac", [("out", 0), ("dve", "c3", 2)], lambda e, i, j: e.activation(row(j % 2, SEQ, 3), ps[:, j % 4, :], ACT.Copy)),
                tap(0), tap(1), tap(2), tap(3),
                ("act", "hi", [("dve", "c3", 0)], lambda e, i, j: e.activation(xc_hi[:, i, :], xc[:, i, :], ACT.Copy), 1),
                ("pool", "lo", [("act", "hi", 0)], lambda e, i, j: e.tensor_tensor(xc_lo[:, i, :], xc[:, i, :], xc_hi[:, i, :].bitcast(F32), ALU.subtract), 1),
            ], width=TOK, after=before, feed=[(h_hi, from_norm(before))], start={"dve": lambda e: zero(e, row(0, 3), row(1, 3))})

        rt_t = z("rt_t", [P, LT, SEQ], L24)
        a_t = z("a_t", [P, LT, SEQ], 2 * L24)
        lam2 = small[:, 0:12]
        lamc = small[:, 112:124]

        class Lambda(Stage):

            def __init__(self, before):
                super().__init__("lam", before)
                self.steps("act", ["ex"])
                self.steps("dve", ["x", "neg", "abs"] + log1p_steps("l") + ["sp", "c", "c2"])

            def act(self, e):
                self.begin(e, "act")
                self.on(e, "dve", 0, "abs")
                self.did("act", e.activation(row(1, LT), row(1, LT), ACT.Exp), "ex")

            def dve(self, e):
                self.begin(e, "dve")
                o = PAR["lam"][0]
                t = [row(r, LT) for r in range(4)]
                self.did("dve", e.tensor_scalar(t[0], par[:, o:o + LT], -1.0, None, ALU.mult), "x")
                self.on(e, "dve", 0, "x")
                self.did("dve", e.tensor_scalar(t[1], t[0], -1.0, None, ALU.mult), "neg")
                self.on(e, "dve", 0, "neg")
                self.did("dve", e.tensor_tensor(t[1], t[1], t[0], ALU.min), "abs")
                self.on(e, "act", 0, "ex")
                log1p(e, self, "l", t[1], t[2], t[3])
                self.did("dve", e.scalar_tensor_tensor(t[0], t[0], 0.0, t[1], ALU.max, ALU.add), "sp")
                self.on(e, "dve", 0, "sp")
                self.did("dve", e.tensor_scalar(lamc, t[0], -4.0, None, ALU.mult), "c")
                self.did("dve", e.tensor_scalar(lam2, t[0], -8.0, None, ALU.mult), "c2")

        def lru(before):
            prog = []
            tiles = []
            for q in range(3):
                tiles += [[(2 * q, lambda j, q=q: 3 * j + q)], [(2 * q + 1, lambda j, q=q: 3 * j + q)]]
            ch = lambda i, q: i * 3 + q
            for q in range(3):
                prog += [
                    ("act", f"r{q}", [("out", 0), ("act", f"e{q}", 1)], lambda e, i, j, q=q: e.activation(row(q), ps[:, 2 * q, :], ACT.Sigmoid, bias=pcol("brg", ch(i, q)))),
                    ("act", f"i{q}", [("dve", f"ix{q}", 1)], lambda e, i, j, q=q: e.activation(row(3 + q), ps[:, 2 * q + 1, :], ACT.Sigmoid, bias=pcol("big", ch(i, q)))),
                    ("dve", f"ix{q}", [("act", f"i{q}", 0)], lambda e, i, j, q=q: e.tensor_tensor(xc[:, ch(i, q), :], row(3 + q), xc[:, ch(i, q), :], ALU.mult)),
                ]
            for q in range(3):
                prog.append(("act", f"t{q}", [("act", f"r{q}", 0)], lambda e, i, j, q=q: e.activation(hs[:, ch(i, q), :], row(q), ACT.Tanh, scale=lamc_col(ch(i, q)))))
            for q in range(3):
                prog.append(("act", f"e{q}", [("act", f"r{q}", 0)], lambda e, i, j, q=q: e.activation(a_t[:, ch(i, q), :], row(q), ACT.Exp, scale=lam2_col(ch(i, q)))))
            prog.append(("act", "rt", [("out", 0), ("act", "t2", 0)], lambda e, i, j: e.activation(rt_t[:], hs[:], ACT.Sqrt, scale=-1.0), "end"))
            return Linear("lru", before, 1, 4, [(0, xc_hi, xc_lo, tiles, True, True)],
                          lambda j, o: [[ps[:, b, :]] for b in range(6)], {0: ("act", "i2", 1)}, prog, width=ALL, after=before, feed=[(xc_hi, from_items(before))])

        def lru_scan(before):
            return Linear("lgate", before, LT // 4, 4, [(0, h_hi, h_lo, K8, True, True)], one(0), {0: ("act", "sg", 4)}, [
                ("act", "sg", [("out", 0), ("dve", "v", 2)], lambda e, i, j: e.activation(row(j % 2), ps[:, j % 4, :], ACT.Silu)),
                ("dve", "a1", [("dve", "a", 1)], lambda e, i, j: e.scalar_tensor_tensor(row(4), a_t[:, i, :], 1.0, hs[:, i, :], ALU.add, ALU.mult)),
                ("dve", "a", [("dve", "a1", 0), ("dve", "h", 1)], lambda e, i, j: e.tensor_scalar(row(6), row(4), 1.0, None, ALU.add)),
                ("dve", "b", [("dve", "a", 0)], lambda e, i, j: e.scalar_tensor_tensor(row(7), row(6), 1.0, rt_t[:, i, :], ALU.add, ALU.mult)),
                ("dve", "bx", [("dve", "b", 0)], lambda e, i, j: e.tensor_tensor(row(7), row(7), xc[:, i, :], ALU.mult)),
                ("dve", "h", [("dve", "bx", 0)], lambda e, i, j: e.tensor_tensor_scan(hs[:, i, :], row(6), row(7), 0.0, ALU.mult, ALU.add)),
                ("dve", "v", [("act", "sg", 0), ("dve", "h", 0), ("pool", "lo", 2)], lambda e, i, j: e.tensor_tensor(row(2 + j % 2), row(j % 2), hs[:, i, :], ALU.mult)),
            ] + split(xc_hi, xc_lo, 2, "v"), width=TOK, after=before)

        def lamc_col(c):
            return small[:, 112:124].rearrange("p (n k) -> p n k", k=1)[:, c, :]

        def lam2_col(c):
            return small[:, 0:12].rearrange("p (n k) -> p n k", k=1)[:, c, :]

        class Output(Stage):
            def __init__(self, before):
                super().__init__("store", before)

            def sp(self, e):
                for k in range(0, KT, 2):
                    self.before.on(e, "dve", 0, ("h", k + 1))
                    e.dma_start(out[:, k:k + 2, :], x[:, k:k + 2, :]).then_inc(s_out, 16)
                e.wait_ge(s_out, 16 * KT // 2)

        pro = Prologue()
        n1 = Norm("norm1", None, x_in, "norm1", T1, hf=hf0, sq=sqv, rr=rrow, acc=cacc[:, 0, :], pro=pro)
        q_ = qkv("q", n1, "cq", qT, None, None)
        k_ = qkv("k", q_, "ck", kT, qT, "ones128")
        v_ = qkv("v", k_, "cv", vT, kT, "ones")
        ga = Gates(v_, pro)
        tu = Turn(ga, v_, ga)
        dc = Decays(tu, ga)
        dm = Delta("dmeta", dc, True)
        dd = Delta("delta", dm, False)
        zz = gate_z(dd)
        sc_ = short_conv(zz)
        bs = branch_sc(sc_)
        bd = branch_dn(bs)
        ou = residual("out", bd, me_hi, me_lo, [8], bd, first=x_res)
        n2 = Norm("norm2", ou, x, "norm2", SEQ)
        gu = gate_up(n2)
        lm = Lambda(gu)
        dn = residual("down", lm, y_hi, y_lo, [8, 8, 6], gu, w0="fin1")
        n3 = Norm("even", dn, x, "even", SEQ, w0="fin1")
        gl = glu_conv(n3)
        bv = PoolDiff(gl)
        pm = pool_mix(bv)
        ag = a_gate(pm)
        bg = b_gate(ag)
        mi = residual("mix", bg, mx_hi, mx_lo, [8, 8], bg, lambda k: (bg, 0, ("alo", k) if k < KT else ("lo", k - KT)))
        n4 = Norm("odd", mi, x, "odd", SEQ)
        xr = lru_conv(n4)
        lr = lru(xr)
        lg = lru_scan(lr)
        lo = residual("lout", lg, xc_hi, xc_lo, [8, 4], lg)
        f2 = Norm("fin2", lo, x, "fin2", SEQ, plain=x)
        Output(f2)

        block = ctx.enter_context(nc.Block())

        @block.sync
        def _(e):
            for s in stages:
                s.sp(e)

        @block.scalar
        def _(e):
            ticks[e] = e.alloc_register("act_tick")
            e.reg_mov(ticks[e], 0)
            for s in stages:
                s.open(e, "act")
            for s in stages:
                s.act(e)

        @block.vector
        def _(e):
            for s in stages:
                s.open(e, "dve")
            for s in stages:
                s.dve(e)

        @block.gpsimd
        def _(e):
            ticks[e] = e.alloc_register("pool_tick")
            e.reg_mov(ticks[e], 0)
            for s in stages:
                s.open(e, "pool")
            for s in stages:
                s.pool(e)

        @block.tensor
        def _(e):
            for s in stages:
                s.open(e, "pe")
            for s in stages:
                s.pe(e)


def tiles_of(w):
    k, m = w.shape
    return w.reshape(k // P, P, m // P, P).transpose(2, 0, 1, 3)


def units_of(groups):
    u = np.zeros((len(groups), WT, P, P), np.float32)
    for n, g in enumerate(groups):
        u[n, :len(g)] = g
    return u.transpose(0, 2, 1, 3).reshape(len(groups), P, WT * P)


def weight_stream(i):
    f = {k: np.asarray(i[k]) for k in i}
    w_in = f["w_in"][0]
    c = np.cumsum([0, D, D, D, D, 16, 16, D, D, D, D, D])
    part = {n: tiles_of(w_in[:, c[j]:c[j + 1]]) for j, n in enumerate(["q", "k", "v", "z", "b", "a", "scb", "scc", "scx", "ga", "gb"]) if n not in "ba"}
    dn, sc, wo = (tiles_of(f[n][0]) for n in ("w_branch_dn", "w_branch_sc", "w_out"))
    gu, down = tiles_of(f["w_gate_up"][0]), tiles_of(f["w_down"][0])
    ev = tiles_of(f["w_in_even_2"][0])
    val, glu, ag, bv, bg = (ev[KT * j:KT * (j + 1)] for j in range(5))
    pw = [tiles_of(f["pool_w_2"][0, g]) for g in range(4)]
    mix, odd, lo = tiles_of(f["w_out_even_2"][0]), tiles_of(f["w_in_odd_2"][0]), tiles_of(f["w_out_odd_2"][0])
    rg, ig = f["w_rg_2"][0], f["w_ig_2"][0]
    s = {
        "q": list(part["q"]), "k": list(part["k"]), "v": list(part["v"]), "z": list(part["z"]),
        "sc": [part[n][t] for t in range(KT) for n in ("scc", "scx", "scb")],
        "bsc": [w[t] for t in range(KT) for w in (part["gb"], sc)],
        "bdn": [w[t] for t in range(KT) for w in (part["ga"], dn)],
        "out": list(wo), "gu": [gu[t + o] for t in range(FT) for o in (0, FT)],
        "down": [down[t, k:k + 8] for t in range(KT) for k in (0, 8, 16)],
        "glu": [w[t] for t in range(KT) for w in (val, glu)], "bval": list(bv),
        "pool": [[pw[g][m, k] for m in range(2) for k in range(2)] for g in range(4)],
        "bgate": list(bg), "agate": list(ag), "mix": [mix[t, k:k + 8] for t in range(KT) for k in (0, 8)],
        "xr": list(odd[:LT]), "lru": [[w[3 * g + q] for q in range(3) for w in (rg, ig)] for g in range(4)],
        "lgate": list(odd[LT:]), "lout": [lo[t, k:k + 8] for t in range(KT) for k in (0, 8)],
    }
    return units_of([u for name, n in UNITS for u in s[name]])


def params(i):
    src = {"norm1": "norm1_w", "sc": "sc_conv_w", "dnn": "dn_norm_w", "norm2": "norm2_w", "fin1": "final_norm_w",
           "even": "norm_even_2", "ca": "conv_a_w_2", "cab": "conv_a_b_2", "lng": "ln_a_g_2", "lnb": "ln_a_b_2",
           "pb": "pool_b_2", "psc": "pool_scale_2", "odd": "norm_odd_2", "cc": "conv_c_w_2", "ccb": "conv_c_b_2",
           "brg": "b_rg_2", "big": "b_ig_2", "lam": "lru_lambda_2", "fin2": "final_norm_2"}
    out = np.zeros((P, NPAR_PAD), np.float32)
    for name, n, k in PARAMS:
        if name in ("cq", "ck", "cv"):
            j = ("cq", "ck", "cv").index(name)
            v = np.asarray(i["dn_conv_w"])[0][:, j * D:(j + 1) * D]
        else:
            v = np.asarray(i[src[name]])
        o = PAR[name][0]
        out[:, o:o + n * k] = v.reshape(k, n, P).transpose(2, 1, 0).reshape(P, n * k)
    return out


def constants():
    r = np.arange(P)
    row, col = r[:, None], r[None, :]
    one = np.ones((P, P), np.float32)
    m = {"ident": row == col, "ones": one, "ones128": one * P, "mean1024": one / D, "mean128": one / P,
         "uf": row <= col, "vf": row > col, "ub": row >= col, "vb": row < col}
    for b in LEVELS:
        m[f"m{b}"] = (row // (2 * b) == col // (2 * b)) & (row // b != col // b)
    cf = np.stack([m[n].astype(np.float32) for n in CONSTS], 1)
    cb = np.stack([m["ident"], NEG * (row > col), NEG * (row < col)], 1).astype(mybir.dt.np(BF16))
    return cf, cb


def kernel(**inputs):
    import concourse.bacc as _bacc
    from concourse.bass_utils import run_bass_kernel_spmd as _run

    i = {k: np.asarray(v) for k, v in inputs.items()}
    cf, cb = constants()
    tok = np.concatenate([i["meta_tokens"], i["x"][0]], 0)
    small = np.ones((P, 128), np.float32)
    small[:, 124:127] = [EPS, P * EPS, 1e-5]
    small[:, 0:16] = i["A_log"].reshape(1, 16)
    small[:, 16:32] = i["dt_bias"].reshape(1, 16)
    for g, w in enumerate(POOLW):
        small[:, 48 + 16 * g:64 + 16 * g] = 1.0 / np.minimum(np.arange(1, 17), w)
    wba = np.zeros((P, KT, P), np.float32)
    wba[:, :, 0:32] = i["w_in"][0][:, 4 * D:4 * D + 32].reshape(KT, P, 32).transpose(1, 0, 2)
    arrays = {
        "x": np.ascontiguousarray(tok.T.reshape(KT, P, T1).transpose(1, 0, 2)),
        "w": weight_stream(i),
        "wba": wba,
        "par": params(i), "cf": cf, "cb": cb, "small": small,
    }
    nc = _bacc.Bacc("TRN2", target_bir_lowering=False, num_devices=1)
    a = {n: nc.dram_tensor(f"in_{n}", v.shape, mybir.dt.from_np(v.dtype), kind="ExternalInput").ap() for n, v in arrays.items()}
    out = nc.dram_tensor("out_0", (P, KT, SEQ), F32, kind="ExternalOutput").ap()
    build(nc, a, out)
    r = _run(nc, [{f"in_{n}": v for n, v in arrays.items()}], core_ids=[0])
    got = r.results[0]["out_0"]
    return np.ascontiguousarray(got.transpose(2, 1, 0).reshape(1, SEQ, D))
```
